# Optimizing a Trainium2 kernel written in Bass

```python
import jax, jax.numpy as jnp
from jax import lax
import numpy as np

D_MODEL = 1024
BATCH = 1
SEQ = 256
DEPTH = 2

CTX_LEN = 256
GRID_W = 64
EPS = 1e-6
D_HGRN = 512
HGRN_HEADS = 4
HGRN_DK = D_HGRN // HGRN_HEADS
HGRN_DV = D_HGRN // HGRN_HEADS
HGRN_SCALE = HGRN_DK ** -0.5
CHUNK = 64
D_POOL = 512
POOL_WINDOWS = (2, 4, 8, 16)
POOL_GROUP = D_POOL // len(POOL_WINDOWS)
IN_COLS = 5 * D_HGRN + D_POOL + 2 * D_MODEL
SPLIT_IDX = (D_HGRN, 2 * D_HGRN, 3 * D_HGRN, 4 * D_HGRN, 5 * D_HGRN, 5 * D_HGRN + D_POOL, 5 * D_HGRN + D_POOL + D_MODEL)
D_FF = 2816
N_EXPERTS = 8
TOP_K = 2
D_EXPERT = 3584
N_DENSE = (DEPTH + 1) // 2
N_MOE = DEPTH // 2

kernel_name = "hybrid_hgrn2_pool_moe_diffusion_trunk"

def rms_norm(x, gain):
    xf = x.astype(jnp.float32)
    y = xf * lax.rsqrt(jnp.mean(xf * xf, axis=-1, keepdims=True) + EPS)
    return (y * gain.astype(jnp.float32)).astype(x.dtype)

def head_rms_norm(o, gain):
    b, n, _ = o.shape
    oh = o.reshape(b, n, HGRN_HEADS, HGRN_DV).astype(jnp.float32)
    oh = oh * lax.rsqrt(jnp.mean(oh * oh, axis=-1, keepdims=True) + EPS)
    return oh.reshape(b, n, D_HGRN) * gain.astype(jnp.float32)

def to_heads(a):
    b, n, _ = a.shape
    return a.reshape(b, n, HGRN_HEADS, -1).transpose(0, 2, 1, 3)

def from_heads(a):
    b, h, n, d = a.shape
    return a.transpose(0, 2, 1, 3).reshape(b, n, h * d)

def flip_seq(a):
    return jnp.flip(a, axis=2)

def forget_gate(z, lb):
    zf = z.astype(jnp.float32)
    lbf = lb.astype(jnp.float32)
    log_f = jnp.logaddexp(jnp.log(lbf), jnp.log1p(-lbf) + jax.nn.log_sigmoid(zf))
    k = (1.0 - lbf) * jax.nn.sigmoid(-zf)
    return log_f, k

def recurrence_inputs(f_fwd, f_bwd, i, lb):
    lf_f, k_f = forget_gate(f_fwd, lb[0])
    lf_b, k_b = forget_gate(f_bwd, lb[1])
    return to_heads(k_f), to_heads(lf_f), to_heads(k_b), to_heads(lf_b), to_heads(i)

def gla_scan(q, k, v, log_f, s0):
    b, h, n, dk = q.shape
    nc = n // CHUNK

    def to_chunks(a):
        return jnp.moveaxis(a.reshape(b, h, nc, CHUNK, a.shape[-1]), 2, 0)

    causal = jnp.tril(jnp.ones((CHUNK, CHUNK), dtype=bool))[:, :, None]

    def step(s, inp):
        qc, kc, vc, gc = inp
        cum = jnp.cumsum(gc.astype(jnp.float32), axis=2)
        o_inter = jnp.einsum('bhtk,bhkv->bhtv', qc * jnp.exp(cum), s)
        diff = cum[:, :, :, None, :] - cum[:, :, None, :, :]
        decay = jnp.exp(jnp.where(causal, diff, -jnp.inf))
        att = jnp.einsum('bhtk,bhsk,bhtsk->bhts', qc, kc, decay)
        o = o_inter + jnp.einsum('bhts,bhsv->bhtv', att, vc)
        last = cum[:, :, -1:, :]
        s_new = jnp.exp(last[:, :, 0, :])[..., None] * s + jnp.einsum('bhsk,bhsv->bhkv', kc * jnp.exp(last - cum), vc)
        return s_new, o

    s_fin, o = lax.scan(step, s0, (to_chunks(q), to_chunks(k), to_chunks(v), to_chunks(log_f)))
    o = jnp.moveaxis(o, 0, 2).reshape(b, h, n, v.shape[-1])
    return o, s_fin

def final_state(k, v, log_f):
    cum = jnp.cumsum(log_f.astype(jnp.float32), axis=2)
    w = jnp.exp(cum[:, :, -1:, :] - cum)
    return jnp.einsum('bhnk,bhnv->bhkv', k * w, v)

def box_mean(x, w, axis):
    length = x.shape[axis]
    cs = jnp.cumsum(x.astype(jnp.float32), axis=axis)
    zero = jnp.zeros_like(lax.slice_in_dim(cs, 0, 1, axis=axis))
    cs = jnp.concatenate([zero, cs], axis=axis)
    pos = jnp.arange(length)
    lo = jnp.clip(pos - w // 2, 0, length)
    hi = jnp.clip(pos - w // 2 + w, 0, length)
    s = jnp.take(cs, hi, axis=axis) - jnp.take(cs, lo, axis=axis)
    cnt = (hi - lo).astype(jnp.float32).reshape((length,) + (1,) * (x.ndim - axis - 1))
    return (s / cnt).astype(x.dtype)

def pool_branch(u, pool_w, pool_scale, on_grid):
    b, n, _ = u.shape
    if on_grid:
        rows = n // GRID_W
        u = u.reshape(b, rows, GRID_W, D_POOL)
    outs = []
    for gi, w in enumerate(POOL_WINDOWS):
        ug = u[..., gi * POOL_GROUP:(gi + 1) * POOL_GROUP]
        m = box_mean(ug, w, 1)
        if on_grid:
            m = box_mean(m, w, 2)
        outs.append(jnp.einsum('...c,ce->...e', m - ug, pool_w[gi]))
    y = jnp.concatenate(outs, axis=-1) * pool_scale
    return y.reshape(b, n, D_POOL)

def token_mixer(h, w_in, lb, o_gain, pool_w, pool_scale, w_br_rec, w_br_pool, w_out, s0_f, s0_b, on_grid):
    p = jnp.einsum('bnd,de->bne', h, w_in)
    q, f_fwd, f_bwd, i, g, u, ga, gb = jnp.split(p, SPLIT_IDX, axis=-1)
    k_f, lf_f, k_b, lf_b, v = recurrence_inputs(f_fwd, f_bwd, i, lb)
    qh = to_heads(jax.nn.silu(q)) * HGRN_SCALE
    o_f, s_f = gla_scan(qh, k_f, v, lf_f, s0_f)
    o_b, s_b = gla_scan(flip_seq(qh), flip_seq(k_b), flip_seq(v), flip_seq(lf_b), s0_b)
    o = from_heads(o_f + flip_seq(o_b))
    y_rec = (head_rms_norm(o, o_gain) * jax.nn.silu(g.astype(jnp.float32))).astype(h.dtype)
    y_pool = pool_branch(u, pool_w, pool_scale, on_grid)
    merged = (jax.nn.sigmoid(ga) * jnp.einsum('bnc,cd->bnd', y_rec, w_br_rec)
              + jax.nn.sigmoid(gb) * jnp.einsum('bnc,cd->bnd', y_pool, w_br_pool))
    return jnp.einsum('bnd,de->bne', merged, w_out), s_f, s_b

def context_states(h, w_in, lb):
    p = jnp.einsum('bnd,de->bne', h, w_in[:, D_HGRN:4 * D_HGRN])
    f_fwd, f_bwd, i = jnp.split(p, 3, axis=-1)
    k_f, lf_f, k_b, lf_b, v = recurrence_inputs(f_fwd, f_bwd, i, lb)
    s_f = final_state(k_f, v, lf_f)
    s_b = final_state(flip_seq(k_b), flip_seq(v), flip_seq(lf_b))
    return s_f, s_b

def swiglu(h, wg, wu, wd):
    return jnp.einsum('bnf,fd->bnd', jax.nn.silu(jnp.einsum('bnd,df->bnf', h, wg)) * jnp.einsum('bnd,df->bnf', h, wu), wd)

def moe_swiglu(h, router, wg, wu, wd):
    logits = jnp.einsum('bnd,de->bne', h, router).astype(jnp.float32)
    top_v, top_i = lax.top_k(logits, TOP_K)
    probs = jax.nn.softmax(top_v, axis=-1)
    gates = jnp.sum(jax.nn.one_hot(top_i, N_EXPERTS, dtype=jnp.float32) * probs[..., None], axis=-2).astype(h.dtype)
    y = jnp.zeros_like(h)
    for e in range(N_EXPERTS):
        y = y + gates[..., e:e + 1] * swiglu(h, wg[e], wu[e], wd[e])
    return y

def channel_mixer(h, l, ffn_w_gate, ffn_w_up, ffn_w_down, moe_router, moe_w_gate, moe_w_up, moe_w_down):
    if l % 2 == 0:
        j = l // 2
        return swiglu(h, ffn_w_gate[j], ffn_w_up[j], ffn_w_down[j])
    j = l // 2
    return moe_swiglu(h, moe_router[j], moe_w_gate[j], moe_w_up[j], moe_w_down[j])

def setup_inputs(seed: int = 0) -> dict:
    key = jax.random.key(seed)
    ks = jax.random.split(key, 32)
    f32 = jnp.float32

    def nrm(k, shape, scale):
        return jax.random.normal(k, shape, f32) * scale

    def gain(k, shape):
        return 1.0 + 0.05 * jax.random.normal(k, shape, f32)

    D = D_MODEL
    return {
        "x": nrm(ks[0], (BATCH, SEQ, D), 1.0),
        "c": nrm(ks[1], (BATCH, D), 1.0),
        "ctx": nrm(ks[2], (BATCH, CTX_LEN, D), 1.0),
        "c_ctx": nrm(ks[3], (D,), 1.0),
        "ada_w": nrm(ks[4], (DEPTH, D, 6 * D), D ** -0.5),
        "ada_b": nrm(ks[5], (DEPTH, 6 * D), 0.02),
        "mix_pre": gain(ks[6], (DEPTH, D)),
        "mix_post": gain(ks[7], (DEPTH, D)),
        "ffn_pre": gain(ks[8], (DEPTH, D)),
        "ffn_post": gain(ks[9], (DEPTH, D)),
        "w_in": nrm(ks[10], (DEPTH, D, IN_COLS), D ** -0.5),
        "hgrn_lb": nrm(ks[11], (DEPTH, 2, D_HGRN), 0.5),
        "hgrn_gain": gain(ks[12], (DEPTH, D_HGRN)),
        "pool_w": nrm(ks[13], (DEPTH, len(POOL_WINDOWS), POOL_GROUP, POOL_GROUP), POOL_GROUP ** -0.5),
        "pool_scale": gain(ks[14], (DEPTH, D_POOL)),
        "w_branch_rec": nrm(ks[15], (DEPTH, D_HGRN, D), D_HGRN ** -0.5),
        "w_branch_pool": nrm(ks[16], (DEPTH, D_POOL, D), D_POOL ** -0.5),
        "w_out": nrm(ks[17], (DEPTH, D, D), D ** -0.5),
        "ffn_w_gate": nrm(ks[18], (N_DENSE, D, D_FF), D ** -0.5),
        "ffn_w_up": nrm(ks[19], (N_DENSE, D, D_FF), D ** -0.5),
        "ffn_w_down": nrm(ks[20], (N_DENSE, D_FF, D), D_FF ** -0.5),
        "moe_router": nrm(ks[21], (N_MOE, D, N_EXPERTS), D ** -0.5),
        "moe_w_gate": nrm(ks[22], (N_MOE, N_EXPERTS, D, D_EXPERT), D ** -0.5),
        "moe_w_up": nrm(ks[23], (N_MOE, N_EXPERTS, D, D_EXPERT), D ** -0.5),
        "moe_w_down": nrm(ks[24], (N_MOE, N_EXPERTS, D_EXPERT, D), D_EXPERT ** -0.5),
    }

def reference(x, c, ctx, c_ctx, ada_w, ada_b, mix_pre, mix_post, ffn_pre, ffn_post, w_in, hgrn_lb, hgrn_gain,
              pool_w, pool_scale, w_branch_rec, w_branch_pool, w_out, ffn_w_gate, ffn_w_up, ffn_w_down,
              moe_router, moe_w_gate, moe_w_up, moe_w_down):
    lb_all = jnp.cumsum(jax.nn.softmax(hgrn_lb.astype(jnp.float32), axis=0), axis=0)
    lb_all = lb_all - lb_all[0:1]
    cx = ctx
    b = x.shape[0]
    for l in range(DEPTH):
        last = l == DEPTH - 1
        mod_x = (jnp.einsum('bd,de->be', jax.nn.silu(c), ada_w[l]) + ada_b[l])[:, None, :]
        sh1, sc1, g1, sh2, sc2, g2 = jnp.split(mod_x, 6, axis=-1)
        mod_c = jnp.einsum('d,de->e', jax.nn.silu(c_ctx), ada_w[l]) + ada_b[l]
        csh1, csc1, cg1, csh2, csc2, cg2 = jnp.split(mod_c, 6, axis=-1)
        mix_params = (w_in[l], lb_all[l], hgrn_gain[l], pool_w[l], pool_scale[l],
                      w_branch_rec[l], w_branch_pool[l], w_out[l])
        ffn_params = (ffn_w_gate, ffn_w_up, ffn_w_down, moe_router, moe_w_gate, moe_w_up, moe_w_down)

        hc = rms_norm(cx, mix_pre[l]) * (1.0 + csc1) + csh1
        if last:
            s_f, s_b = context_states(hc, w_in[l], lb_all[l])
        else:
            s0 = jnp.zeros((b, HGRN_HEADS, HGRN_DK, HGRN_DV), jnp.float32)
            yc, s_f, s_b = token_mixer(hc, *mix_params, s0, s0, False)
            cx = cx + cg1 * rms_norm(yc, mix_post[l])
        hx = rms_norm(x, mix_pre[l]) * (1.0 + sc1) + sh1
        yx, _, _ = token_mixer(hx, *mix_params, s_f, s_b, True)
        x = x + g1 * rms_norm(yx, mix_post[l])

        hx2 = rms_norm(x, ffn_pre[l]) * (1.0 + sc2) + sh2
        x = x + g2 * rms_norm(channel_mixer(hx2, l, *ffn_params), ffn_post[l])
        if not last:
            hc2 = rms_norm(cx, ffn_pre[l]) * (1.0 + csc2) + csh2
            cx = cx + cg2 * rms_norm(channel_mixer(hc2, l, *ffn_params), ffn_post[l])
    return x


_drawn_inputs = setup_inputs


def setup_inputs(seed=0):
    import zlib

    import numpy as np

    out = dict(_drawn_inputs(seed))
    spreads = {}
    factors = {'ctx': 7.288, 'c_ctx': 2.911, 'hgrn_lb': 5.35}
    for name, (base, spread) in spreads.items():
        noise = np.random.default_rng([zlib.crc32(name.encode()), seed]).standard_normal(out[name].shape)
        drawn = base * np.exp(spread * noise) if base else spread * noise
        out[name] = __import__('jax').numpy.asarray(drawn.astype(out[name].dtype))
    for name, factor in factors.items():
        out[name] = (out[name] * factor).astype(out[name].dtype)
    return out
```

```python
from contextlib import ExitStack

import concourse.bass as bass
from concourse import mybir

F32 = mybir.dt.float32
F32R = mybir.dt.float32r
I32 = mybir.dt.int32
U32 = mybir.dt.uint32
U8 = mybir.dt.uint8
ALU = mybir.AluOpType
ACT = mybir.ActivationFunctionType
AX = mybir.AxisListType

P = 128
D = 1024
KT = D // P
S = 256
T = 2 * S
ROWS, GRID_W = 4, 64
HEADS = 4
HS = 128.0 ** -0.5
EPS = 1e-6
F_DENSE, F_EXP, NE = 2816, 3584, 8
FT = F_DENSE // P
LEVELS = [1 << i for i in range(8)]
POOL_PAD = 8
JOBS = 11
UC = 256
STEPS = F_EXP // 256
ORDER = []
for _st in range(STEPS):
    ORDER += [("A", _st), ("B", _st)] + ([("D", _st - 2)] if _st >= 2 else [])
ORDER += [("D", STEPS - 2), ("D", STEPS - 1)]
JU = len(ORDER)
RAW_M, HL_M = 6, 3
IN_ORDER = [1, 2, 5, 3, 4, 0, 6, 7, 8, 9]
N_IN, N_BR, N_OUT, N_GU, N_DN = 20, 4, 4, 2 * F_DENSE // UC, 12
ADA_UNITS = 48
L0_UNITS = N_IN + N_BR + N_OUT + N_GU + N_DN
DENSE_UNITS = L0_UNITS + N_IN + N_BR + N_OUT


def misc_plan():
    table, used, n = {}, [0, 0, 0, 0], [0]

    def add(name):
        b = n[0] % 4
        table[name] = (b, n[0] + 1, used[b])
        used[b] += 1
        n[0] += 1

    for k in range(KT):
        add(("xT", k))
    add("prmA")
    add("prmB")
    for i in range(ADA_UNITS):
        add(("ada", i))
    for l in range(2):
        add(("ms", l, "mix_pre"))
        for g in range(4):
            add(("pool", l, g))
        for s in range(2):
            full = l == 0 or s == 1
            if full:
                add(("diag", l, s, 0))
                add(("diag", l, s, 1))
            for d in range(2):
                if full:
                    for li, h in enumerate(LEVELS):
                        for tt in range(2 if h < P else 1):
                            add(("att", l, s, d, li, tt))
                if s == 0:
                    add(("kT", l, d, 0))
                    add(("kT", l, d, 1))
                    add(("st", l, d))
            if full:
                for i in range(2):
                    add(("o", l, s, i))
                for i in range(2):
                    add(("oms", l, s, i))
        add(("ms", l, "mix_post"))
        add(("ms", l, "ffn_pre"))
        if l == 0:
            add(("ms", l, "ffn_post"))
    for t in range(2):
        add(("logit", t))
    for i in range(4):
        add(("h2", i))
    add("rank")
    add("gslot")
    for j in range(JOBS):
        add(("pT", j))
    return table, n[0], used


MISC, MISC_N, MISC_USED = misc_plan()


class Steps:

    def __init__(self, eng, sem):
        self.eng, self.sem, self.base, self.k = eng, sem, 0, 0

    def mark(self, ins):
        ins.then_inc(self.sem, 1)
        self.k += 1

    def sync(self):
        self.eng.wait_ge(self.sem, self.base + self.k)

    def step(self, ins):
        self.mark(ins)
        self.sync()

    def enter(self, i, per):
        self.start = self.base + self.k
        self.per = per
        self.base, self.k = self.start + i * per, 0

    def leave(self, n):
        assert self.k == self.per, (self.k, self.per)
        self.base, self.k = self.start + n * self.per, 0


VM = 1408
VK = 6


def trunk_kernel(nc, A, out):
    with ExitStack() as ctx:
        base = (nc.sbuf_base + 63) // 64 * 64
        at = [base]

        def place(name, shape, dt, offset=None):
            size = 1 if dt == U8 else 4
            for n in shape[1:]:
                size *= n
            size = (size + 31) // 32 * 32
            if offset is None:
                offset = at[0]
                at[0] += size
            assert offset + size <= nc.sbuf_usable_end, (name, offset + size, nc.sbuf_usable_end)
            return nc.alloc_sbuf_tensor_at(name, shape, dt, offset=offset)

        K8 = 8192
        ident = place("ident", [P, P], F32)
        ones_d = place("ones_d", [P, P], F32)
        ones_h = place("ones_h", [P, P], F32)
        eps_t = place("eps_t", [P, 1], F32)
        masks = place("masks", [P, 14, P], U8)
        mod = place("mod", [P, 2, 48, 2], F32)
        prm = place("prm", [P, 96], F32)
        adab = place("adab", [P, 96], F32)
        lbp = place("lbp", [P, 6, 8], F32)
        poolw = place("poolw", [P, 4, P], F32)
        csil = place("csil", [P, KT, 2], F32)
        craw = place("craw", [P, 2, KT], F32)
        rstd = place("rstd", [P, T], F32)
        state = place("state", [P, 2, HEADS, P], F32)
        R = place("R", [P, KT, T], F32)
        ring0 = at[0]
        raw = [place(f"raw{i}", [P, KT, UC], F32) for i in range(2)]
        w_hi = [place(f"w_hi{i}", [P, KT, UC], F32R) for i in range(2)]
        w_lo = [place(f"w_lo{i}", [P, KT, UC], F32R) for i in range(2)]
        h0 = at[0]
        h_hi = place("h_hi", [P, KT, T], F32R)
        h_lo = place("h_lo", [P, KT, T], F32R)
        z0 = at[0]
        q = place("q", [P, 2, HEADS, S], F32)
        lf = place("lf", [P, 2, 2, HEADS, S], F32)
        kk = place("kk", [P, 2, 2, HEADS, S], F32)
        v = place("v", [P, 4, 512], F32)
        g = place("g", [P, HEADS, T], F32)
        u = place("u", [P, HEADS, T], F32)
        x0 = at[0]
        cA = place("cA", [P, HEADS, S], F32)
        cB = place("cB", [P, HEADS, S], F32)
        QE = [place(f"QE{i}", [P, HEADS, S], F32) for i in range(2)]
        KE = [place(f"KE{i}", [P, HEADS, S], F32) for i in range(2)]
        att = place("att", [P, 2, HEADS, S], F32)
        end = at[0]
        gE = place("gE", [P, 2, HEADS, S], F32, x0 + 8192)
        gL = place("gL", [P, 2, HEADS, S], F32, x0 + 16384)
        invc = place("invc", [P, 4, T], F32, x0 + 24576)
        pads = [place(f"pad{i}", [P, 1024], F32, x0 + 4096 * i) for i in range(2)]
        gate_st = [place(f"gate_st{i}", [P, T], F32, x0 + 8192 + 2048 * i) for i in range(2)]
        yr_hi = place("yr_hi", [P, 4, T], F32R, h0)
        yr_lo = place("yr_lo", [P, 4, T], F32R, h0 + K8)
        yp_hi = place("yp_hi", [P, 4, T], F32R, h0 + 2 * K8)
        yp_lo = place("yp_lo", [P, 4, T], F32R, h0 + 3 * K8)
        m_hi = place("m_hi", [P, KT, T], F32R, z0)
        m_lo = place("m_lo", [P, KT, T], F32R, z0 + 2 * K8)
        sgate = [place(f"sgate{i}", [P, 2, 2, T], F32, z0 + 4 * K8 + K8 * i) for i in range(2)]
        mt = [place(f"mt{i}", [P, T], F32, z0 + 6 * K8 + 2048 * i) for i in range(4)]
        Y = place("Y", [P, KT, T], F32, z0 + 8 * K8)
        SQ = place("SQ", [P, KT, T], F32, z0 + 10 * K8)
        HF = SQ
        hid_hi = place("hid_hi", [P, FT, T], F32R, z0)
        hid_lo = place("hid_lo", [P, FT, T], F32R, z0 + 2048 * FT)
        sg = place("sg", [P, 2, T], F32, z0 + 4096 * FT)
        hf = place("hf", [P, 2, T], F32, z0 + 4096 * FT + 4096)
        Y2 = place("Y2", [P, KT, T], F32, h0)
        SQ2 = place("SQ2", [P, KT, T], F32, h0 + 2 * K8)
        xin = place("xin", [P, 4, D], F32, h0)
        rowsA = place("rowsA", [96, P], F32, h0 + 2 * K8)
        rowsB = place("rowsB", [96, P], F32, h0 + 2 * K8 + 512)
        masks_f = place("masks_f", [P, 14, P], F32, z0 + 4 * K8)
        ada_w = [place(f"ada_w{i}", [P, KT, UC], F32, z0 + K8 * i) for i in range(4)]
        raw_m = [place(f"raw_m{i}", [P, 2048], F32, ring0 + K8 * i) for i in range(RAW_M)]
        m0 = h0
        mw_hi = [place(f"mw_hi{i}", [P, 2048], F32R, m0 + K8 * 2 * i) for i in range(HL_M)]
        mw_lo = [place(f"mw_lo{i}", [P, 2048], F32R, m0 + K8 * (2 * i + 1)) for i in range(HL_M)]
        mo = [m0 + 2 * K8 * HL_M]

        def moe(name, shape, dt):
            size = 4
            for n in shape[1:]:
                size *= n
            t = place(name, shape, dt, mo[0])
            mo[0] += size
            assert mo[0] <= end
            return t

        one_hot = moe("one_hot", [P, 2, JOBS + 1, P], F32R)
        scat = moe("scat", [P, JOBS + 1, S], F32R)
        acc = moe("acc", [P, KT, S], F32)
        h2_hi = moe("h2_hi", [P, 2, D], F32R)
        h2_lo = moe("h2_lo", [P, 2, D], F32R)
        xg_hi = moe("xg_hi", [P, KT, P], F32R)
        xg_lo = moe("xg_lo", [P, KT, P], F32R)
        he = [moe(f"he{i}", [P, 256], F32) for i in range(2)]
        sge = [moe(f"sge{i}", [P, 256], F32) for i in range(2)]
        ht_hi = [moe(f"ht_hi{i}", [P, 2, P], F32R) for i in range(2)]
        ht_lo = [moe(f"ht_lo{i}", [P, 2, P], F32R) for i in range(2)]
        ye_hi = moe("ye_hi", [P, D], F32R)
        ye_lo = moe("ye_lo", [P, D], F32R)
        HM = place("HM", [P, KT, S], F32, m0)
        rt0 = m0 + K8
        rw = place("rw", [P, KT, NE], F32, rt0)
        ltri = place("ltri", [P, P], F32, rt0 + 512)
        iota = place("iota", [P, P], F32, rt0 + 1024)
        ones_1 = place("ones_1", [P, P], F32, rt0 + 1536)
        lg = place("lg", [P, 2, NE], F32, rt0 + 2048)
        top_v = place("top_v", [P, 2, 8], F32, rt0 + 2112)
        top_i = place("top_i", [P, 2, 8], U32, rt0 + 2176)
        top_f = place("top_f", [P, 2, 8], F32, rt0 + 2240)
        sel = place("sel", [P, 2, NE], F32, rt0 + 2304)
        gates = place("gates", [P, 2, 12], F32, rt0 + 2368)
        keys = place("keys", [P, 2, 12], F32, rt0 + 2464)
        tmp8 = place("tmp8", [P, 8, NE], F32, rt0 + 2560)
        tmp1 = place("tmp1", [P, 32], F32, rt0 + 2816)
        gslot = place("gslot", [P, 12], F32, None)
        jobs_f = place("jobs_f", [P, 12], F32, rt0 + 3072)
        jobs = place("jobs", [P, 16], I32, None)
        fin = place("fin", [P, 2, D], F32, h0)
        SQM = place("SQM", [P, KT, S], F32, m0 + 2 * K8 * HL_M + 32768)

        pj = [ctx.enter_context(nc.psum_tensor(f"pj{i}", [P, 512], F32)) for i in range(4)]
        mi = [ctx.enter_context(nc.psum_tensor(f"mi{i}", [P, 512], F32)) for i in range(4)]

        names = {}

        def sem(name):
            if name not in names:
                names[name] = ctx.enter_context(nc.semaphore(name))
            return names[name]

        unit_used = sem("unit_used")
        hi_done, lo_dve, lo_pool = sem("hi_done"), sem("lo_dve"), sem("lo_pool")
        raw_in = [sem(f"raw_in{i}") for i in range(2)]
        rawm_in = [sem(f"rawm_in{i}") for i in range(RAW_M)]
        pj_free = [sem(f"pj_free{i}") for i in range(4)]
        mi_free = [sem(f"mi_free{i}") for i in range(4)]
        mi_full = sem("mi_full")

        def mi_of(name):
            b, full, before = MISC[name]
            return mi[b], mi_free[b], full, before

        def kept_keys(d):
            return kk[:, d, 0].rearrange("p e t -> p (e t)").rearrange("p (t e n) -> p t e n", t=2, e=HEADS)

        C0 = [0, S]
        NT = [T, S]
        U_IN, U_BR, U_OUT = ([b + x for b in (0, L0_UNITS)] for x in (0, N_IN, N_IN + N_BR))
        U_GU = N_IN + N_BR + N_OUT
        U_DN = U_GU + N_GU
        L0_ROUNDS = 10 + 4 + 2 + 11 + 2
        R_IN, R_BR, R_OUT = ([b + x for b in (0, L0_ROUNDS)] for x in (0, 10, 14))
        R_GU, R_DN = 16, 27
        LAST_UNIT = DENSE_UNITS - 1
        SCANS = [(l, s, d) for l in range(2) for s in range(2) for d in range(2)]
        FULL = {(l, s): l == 0 or s == 1 for l in range(2) for s in range(2)}

        def number(keep):
            keys = [k + (li,) for k in SCANS for li in range(9) if keep(*k, li)]
            return {k: n + 1 for n, k in enumerate(keys)}

        N_EXP = number(lambda l, s, d, li: FULL[l, s] or li == 8)
        N_Q = number(lambda l, s, d, li: FULL[l, s] and (li < 8 or s == 1))
        N_K = number(lambda l, s, d, li: (FULL[l, s] and li < 8) or (s == 0 and li == 8))

        spill = A["spill"]
        w_in_src = A["w_in"].rearrange("l (k p) n -> l p k n", p=P)
        rec_src = A["w_branch_rec"].rearrange("l (k p) n -> l p k n", p=P)
        pool_src = A["w_branch_pool"].rearrange("l (k p) n -> l p k n", p=P)
        out_src = A["w_out"].rearrange("l (k p) n -> l p k n", p=P)
        gate_src = A["ffn_w_gate"].rearrange("l (k p) n -> l p k n", p=P)[0]
        up_src = A["ffn_w_up"].rearrange("l (k p) n -> l p k n", p=P)[0]
        down_src = A["ffn_w_down"].rearrange("l (k p) n -> l p k n", p=P)[0]
        ada_src = A["ada_w"].rearrange("l (p k) n -> l p k n", k=KT)
        eg_src = A["moe_w_gate"][0]
        eu_src = A["moe_w_up"][0]
        ed_src = A["moe_w_down"][0]

        block = ctx.enter_context(nc.Block())

        @block.sync
        def _(eng):
            for t in range(4):
                src = (A["ctx"], A["x"])[t // 2][0, (t % 2) * P:(t % 2 + 1) * P, :]
                eng.dma_start(xin[:, t, :], src).then_inc(sem("x_in"), 16)
            eng.dma_start(ident[:], A["k_ident"]).then_inc(sem("consts_in"), 16)
            eng.dma_start(masks_f[:], A["k_masks"]).then_inc(sem("consts_in"), 16)
            eng.dma_start(rowsA[:], A["ada_b"].rearrange("l (c p) -> (l c) p", p=P)).then_inc(sem("rows_in"), 16)
            row = 0
            for name in ("mix_pre", "mix_post", "ffn_pre", "ffn_post", "hgrn_lb", "hgrn_gain", "pool_scale"):
                src = A[name]
                if name == "hgrn_lb":
                    src = src.rearrange("l d (c p) -> (l d c) p", p=P)
                else:
                    src = src.rearrange("l (c p) -> (l c) p", p=P)
                eng.dma_start(rowsB[row:row + src.shape[0], :], src).then_inc(sem("rows_in"), 16)
                row += src.shape[0]
            eng.dma_start(craw[:, 0, :], A["c_ctx"].rearrange("(p k) -> p k", k=KT)).then_inc(sem("c_in"), 16)
            eng.dma_start(craw[:, 1, :], A["c"].rearrange("b (p k) -> p (b k)", k=KT)).then_inc(sem("c_in"), 16)

            def ada(l, i, s, first):
                if not first:
                    eng.wait_ge(mi_full, MISC[("ada", 0)][1] + l * 24 + 4 * i + s - 4)
                eng.dma_start(ada_w[s][:], ada_src[l][:, :, bass.ds((4 * i + s) * UC, UC)])\
                   .then_inc(sem(f"ada_in{s}"), 16)

            for s in range(4):
                ada(0, 0, s, True)
            with eng.Fori(1, 6) as i:
                for s in range(4):
                    ada(0, i, s, False)
            with eng.Fori(0, 6) as i:
                for s in range(4):
                    ada(1, i, s, False)

            def load(pair, p, parts):
                if not isinstance(pair, int) or pair > 0:
                    eng.wait_ge(lo_dve, 2 * pair + p - 1)
                    eng.wait_ge(lo_pool, 2 * pair + p - 1)
                k = 0
                for n, (src, kts) in enumerate(parts):
                    eng.dma_start(raw[p][:, k:k + kts, :], src)\
                       .then_inc(raw_in[p], 16 if n < len(parts) - 1 else 16 * (3 - len(parts)))
                    k += kts

            def load_gates(l, b):
                if b == 0:
                    for i in range(2):
                        eng.wait_ge(sem(f"spilled{i}"), 16 * 8 * (l + 1))
                    eng.wait_ge(sem("branches_cut"), 4 * (l + 1))
                if b >= 2:
                    eng.wait_ge(pj_free[3], R_BR[l] + b - 1)
                for i in range(2):
                    eng.dma_start(sgate[b % 2][:, i, :, 0:NT[l]],
                                  spill[8 * i + 2 * b:8 * i + 2 * b + 2, :, 0:NT[l]].rearrange("t p n -> p t n"))\
                       .then_inc(sem(f"gates_in{b % 2}"), 16)

            for l in range(2):
                if l == 0:
                    eng.dma_start(poolw[:], A["pool_w"][0].rearrange("g c e -> c g e")).then_inc(sem("poolw_in"), 16)
                for i in range(6):
                    for p in range(2):
                        c = IN_ORDER[i] * 2 * UC + p * UC
                        load(U_IN[l] // 2 + i, p, [(w_in_src[l][:, :, c:c + UC], KT)])
                with eng.Fori(6, N_IN // 2) as i:
                    for p in range(2):
                        load(U_IN[l] // 2 + i, p, [(w_in_src[l][:, :, bass.ds((2 * i + p) * UC, UC)], KT)])
                for b in range(N_BR):
                    cols = slice(b * UC, (b + 1) * UC)
                    load((U_BR[l] + b) // 2, b % 2, [(rec_src[l][:, :, cols], 4), (pool_src[l][:, :, cols], 4)])
                    if b >= 1:
                        load_gates(l, b - 1)
                load_gates(l, 3)
                if l == 0:
                    eng.wait_ge(mi_full, MISC[("pool", 0, 3)][1])
                    eng.dma_start(poolw[:], A["pool_w"][1].rearrange("g c e -> c g e")).then_inc(sem("poolw_in"), 16)
                for n in range(N_OUT):
                    load((U_OUT[l] + n) // 2, n % 2, [(out_src[l][:, :, n * UC:(n + 1) * UC], KT)])
                if l == 0:
                    with eng.Fori(0, N_GU // 2) as i:
                        load(U_GU // 2 + i, 0, [(gate_src[:, :, bass.ds(i * UC, UC)], KT)])
                        load(U_GU // 2 + i, 1, [(up_src[:, :, bass.ds(i * UC, UC)], KT)])
                    with eng.Fori(0, 2) as i:
                        for n in range(6):
                            k0, kts = 8 * (n % 3), (8, 8, 6)[n % 3]
                            load(U_DN // 2 + 3 * i + n // 2, n % 2,
                                 [(down_src[:, k0:k0 + kts, bass.ds((2 * i + n // 3) * UC, UC)], kts)])

            eng.wait_ge(unit_used, DENSE_UNITS)
            eng.dma_start(rw[:], A["moe_router"][0].rearrange("(k p) e -> p k e", p=P)).then_inc(sem("route_in"), 16)
            eng.dma_start(ltri[:], A["k_ltri"]).then_inc(sem("route_in"), 16)
            eng.dma_start(iota[:], A["k_iota"]).then_inc(sem("route_in"), 16)
            eng.wait_ge(sem("jobs_ready"), 1)
            n_jobs = eng.value_load(jobs[0:1, 0:1], min_val=NE, max_val=JOBS)
            with eng.Fori(0, n_jobs) as j:
                expert = eng.value_load(jobs[0:1, bass.ds(j + 1, 1)], min_val=0, max_val=NE - 1)
                for n, (kind, st) in enumerate(ORDER):
                    slot = raw_m[n % RAW_M]
                    eng.wait_ge(lo_dve, DENSE_UNITS + j * JU + n - RAW_M + 1)
                    eng.wait_ge(lo_pool, DENSE_UNITS + j * JU + n - RAW_M + 1)
                    if kind == "D":
                        src = ed_src[bass.ds(expert, 1), st * 256:(st + 1) * 256, :]\
                            .rearrange("e (k p) n -> p (e k) n", p=P)
                        eng.dma_start(slot[:].rearrange("p (k n) -> p k n", k=2), src)\
                           .then_inc(rawm_in[n % RAW_M], 32)
                    else:
                        k0 = 0 if kind == "A" else 512
                        dst = slot[:].rearrange("p (k h n) -> p k h n", k=4, h=2)
                        for half, w in enumerate((eg_src, eu_src)):
                            src = w[bass.ds(expert, 1), k0:k0 + 512, st * 256:(st + 1) * 256]\
                                .rearrange("e (k p) n -> p (e k) n", p=P)
                            eng.dma_start(dst[:, :, half, :], src).then_inc(rawm_in[n % RAW_M], 16)
            eng.wait_ge(sem("fin_done"), 4)
            for t in range(2):
                eng.dma_start(out[0, t * P:(t + 1) * P, :], fin[:, t, :]).then_inc(sem("stored"), 16)
            eng.wait_ge(sem("stored"), 32)

        @block.tensor
        def _(eng):
            told = [0]

            def tile(name):
                bank, free, full, before = mi_of(name)
                assert full == told[0] + 1, name
                if before:
                    eng.wait_ge(free, before)
                return bank

            def filled(ins):
                ins.then_inc(mi_full, 1)
                told[0] += 1

            eng.wait_ge(sem("x_in"), 64)
            eng.wait_ge(sem("consts_in"), 32)
            for k in range(KT):
                bank = tile(("xT", k))
                for t in range(4):
                    ins = eng.transpose(bank[:, t * P:(t + 1) * P], xin[:, t, k * P:(k + 1) * P], ident[:])
                filled(ins)
            eng.wait_ge(sem("rows_in"), 16 * 8)
            filled(eng.transpose(tile("prmA")[:, 0:96], rowsA[:], ident[0:96, 0:96]))
            filled(eng.transpose(tile("prmB")[:, 0:96], rowsB[:], ident[0:96, 0:96]))
            eng.wait_ge(sem("csil_done"), 1)
            b0, f0, u0 = MISC[("ada", 0)]
            with eng.Fori(0, ADA_UNITS // 4) as i:
                for s in range(4):
                    b = (b0 + s) % 4
                    eng.wait_ge(mi_free[b], MISC[("ada", s)][2] + i)
                    eng.wait_ge(sem(f"ada_in{s}"), 16 * i + 16)
                    for c in range(2):
                        for k in range(KT):
                            ins = eng.matmul(mi[b][:, 2 * c:2 * c + 2], ada_w[s][:, k, c * P:(c + 1) * P],
                                             csil[:, k, :], start=(k == 0), stop=(k == KT - 1))
                    ins.then_inc(mi_full, 1)
            told[0] += ADA_UNITS

            def passes(dst, ah, al, bh, bl, first, last):
                eng.matmul(dst, ah, bh, start=first, stop=False)
                eng.matmul(dst, ah, bl, start=False, stop=False)
                return eng.matmul(dst, al, bh, start=False, stop=last)

            def unit_in(pair, p):
                eng.wait_ge(lo_dve, 2 * pair + p + 1)
                eng.wait_ge(lo_pool, 2 * pair + p + 1)

            def bank_free(b, rounds):
                if not isinstance(rounds, int) or rounds > 0:
                    eng.wait_ge(pj_free[b], rounds)

            def project(pair, rounds, c0, n, xh=h_hi, xl=h_lo):
                for p in range(2):
                    unit_in(pair, p)
                    for j in range(2):
                        bank_free(2 * p + j, rounds)
                        for k in range(KT):
                            w = slice(j * P, (j + 1) * P)
                            ins = passes(pj[2 * p + j][:, 0:n], w_hi[p][:, k, w], w_lo[p][:, k, w],
                                         xh[:, k, c0:c0 + n], xl[:, k, c0:c0 + n], k == 0, k == KT - 1)
                    ins.then_inc(unit_used, 1)

            def project_tokens(pair, rounds):
                for p in range(2):
                    unit_in(pair, p)
                    for t in range(4):
                        if p == 0:
                            bank_free(t, rounds)
                        for k in range(KT):
                            x = slice(t * P, (t + 1) * P)
                            ins = passes(pj[t][:, p * UC:(p + 1) * UC], h_hi[:, k, x], h_lo[:, k, x],
                                         w_hi[p][:, k, :], w_lo[p][:, k, :], k == 0, k == KT - 1)
                    ins.then_inc(unit_used, 1)

            def mean_square(name, sq, c0, n, seen):
                bank = tile(name)
                for k in range(KT):
                    eng.wait_ge(sem("squared"), seen + k + 1)
                    ins = eng.matmul(bank[:, 0:n], ones_d[:], sq[:, k, c0:c0 + n], start=(k == 0), stop=(k == KT - 1))
                filled(ins)

            def scan_products(l, s, d):
                if FULL[l, s]:
                    for li, h in enumerate(LEVELS):
                        eng.wait_ge(sem("q_ready"), N_Q[l, s, d, li])
                        eng.wait_ge(sem("k_ready"), N_K[l, s, d, li])
                        qe, ke = QE[li % 2], KE[li % 2]
                        for tt in range(2 if h < P else 1):
                            bank = tile(("att", l, s, d, li, tt))
                            st, qt = (tt, tt) if h < P else ((0, 1) if d == 0 else (1, 0))
                            for hd in range(HEADS):
                                ins = eng.matmul(bank[:, hd * P:(hd + 1) * P], ke[:, hd, st * P:(st + 1) * P],
                                                 qe[:, hd, qt * P:(qt + 1) * P], start=True, stop=True)
                            filled(ins)
                if s == 0:
                    eng.wait_ge(sem("k_ready"), N_K[l, s, d, 8])
                    for t in range(2):
                        bank = tile(("kT", l, d, t))
                        for hd in range(HEADS):
                            ins = eng.transpose(bank[:, hd * P:(hd + 1) * P], KE[0][:, hd, t * P:(t + 1) * P], ident[:])
                        filled(ins)
                    b1, _, kept1 = MISC[("kT", l, d, 1)]
                    eng.wait_ge(mi_free[b1], kept1 + 1)
                    bank = tile(("st", l, d))
                    for hd in range(HEADS):
                        for t in range(2):
                            ins = eng.matmul(bank[:, hd * P:(hd + 1) * P], kept_keys(d)[:, t, hd, :],
                                             v[:, t, hd * P:(hd + 1) * P], start=(t == 0), stop=(t == 1))
                    filled(ins)

            def token_mix(l):
                c0, n = C0[l], NT[l]
                eng.wait_ge(sem("poolw_in"), 16 * (l + 1))
                eng.wait_ge(sem("pooled"), 4 * (l + 1))
                for gi in range(4):
                    filled(eng.matmul(tile(("pool", l, gi))[:, 0:n], poolw[:, gi, :], u[:, gi, c0:c0 + n],
                                      start=True, stop=True))
                for s in range(2):
                    if FULL[l, s]:
                        eng.wait_ge(sem("diag_q"), l + s + 1 if l == 0 else 3)
                        eng.wait_ge(sem("diag_k"), l + s + 1 if l == 0 else 3)
                        for t in range(2):
                            bank = tile(("diag", l, s, t))
                            for hd in range(HEADS):
                                ins = eng.matmul(bank[:, hd * P:(hd + 1) * P], KE[1][:, hd, t * P:(t + 1) * P],
                                                 QE[1][:, hd, t * P:(t + 1) * P], start=True, stop=True)
                            filled(ins)
                    for d in range(2):
                        scan_products(l, s, d)
                    if not FULL[l, s]:
                        continue
                    ba, _, before = MISC[("att", l, s, 1, 7, 0)]
                    eng.wait_ge(mi_free[ba], before + 1)
                    if s == 1:
                        bs, _, before = MISC[("st", l, 1)]
                        eng.wait_ge(mi_free[bs], before + 1)
                        eng.wait_ge(sem("q_ready"), N_Q[l, s, 1, 8])
                    for i in range(2):
                        bank = tile(("o", l, s, i))
                        for hd in (2 * i, 2 * i + 1):
                            dst = bank[:, (hd % 2) * S:(hd % 2 + 1) * S]
                            for t in range(2):
                                ins = eng.matmul(dst, v[:, 2 * s + t, hd * P:(hd + 1) * P], att[:, t, hd, :],
                                                 start=(t == 0), stop=(t == 1 and s == 0))
                            if s == 1:
                                for d in range(2):
                                    ins = eng.matmul(dst, state[:, d, hd, :], lf[:, d, 1, hd, :],
                                                     start=False, stop=(d == 1))
                        filled(ins)
                    for i in range(2):
                        eng.wait_ge(sem("o_squared"), 2 * (l + s if l == 0 else 2) + i + 1)
                        bank = tile(("oms", l, s, i))
                        filled(eng.matmul(bank[:], ones_h[:], cA[:, 2 * i:2 * i + 2, :].rearrange("p h t -> p (h t)"),
                                          start=True, stop=True))

            SQ_SEEN = {(0, "mix_pre"): 0, (0, "mix_post"): 8, (0, "ffn_pre"): 16, (0, "ffn_post"): 24,
                       (1, "mix_pre"): 32, (1, "mix_post"): 40, (1, "ffn_pre"): 48}
            eng.wait_ge(sem("ones_set"), 3)
            for l in range(2):
                c0, n = C0[l], NT[l]
                mean_square(("ms", l, "mix_pre"), SQ, 0, T, SQ_SEEN[l, "mix_pre"])
                eng.wait_ge(sem("h_cut"), 8 * (2 * l + 1))
                up, ur = U_IN[l] // 2, R_IN[l]
                with eng.Fori(0, 2) as i:
                    project(up + i, ur + i, 0, T)
                project(up + 2, ur + 2, c0, n)
                project_tokens(up + 3, ur + 3)
                with eng.Fori(4, 6) as i:
                    project(up + i, ur + i, c0, n)
                token_mix(l)
                with eng.Fori(6, 10) as i:
                    project(up + i, ur + i, c0, n)
                eng.wait_ge(sem("branches_cut"), 4 * (l + 1))
                for b in range(N_BR):
                    unit_in((U_BR[l] + b) // 2, b % 2)
                    for br, (yh, yl) in enumerate(((yr_hi, yr_lo), (yp_hi, yp_lo))):
                        for j in range(2):
                            bank_free(2 * br + j, R_BR[l] + b)
                            for k in range(4):
                                w = (slice(None), 4 * br + k, slice(j * P, (j + 1) * P))
                                ins = passes(pj[2 * br + j][:, 0:n], w_hi[b % 2][w], w_lo[b % 2][w],
                                             yh[:, k, c0:c0 + n], yl[:, k, c0:c0 + n], k == 0, k == 3)
                    ins.then_inc(unit_used, 1)
                eng.wait_ge(sem("m_cut"), 8 * (l + 1))
                for i in range(2):
                    project(U_OUT[l] // 2 + i, R_OUT[l] + i, c0, n, m_hi, m_lo)
                mean_square(("ms", l, "mix_post"), SQ, c0, n, SQ_SEEN[l, "mix_post"])
                mean_square(("ms", l, "ffn_pre"), SQ, c0, n, SQ_SEEN[l, "ffn_pre"])
                if l == 0:
                    eng.wait_ge(sem("h_cut"), 16)
                    with eng.Fori(0, N_GU // 2) as i:
                        project(U_GU // 2 + i, R_GU + i, 0, T)
                    eng.wait_ge(sem("hid_cut"), FT)
                    with eng.Fori(0, 2) as i:
                        for n6 in range(6):
                            gr, pc = n6 // 3, n6 % 3
                            unit_in(U_DN // 2 + 3 * i + n6 // 2, n6 % 2)
                            for j in range(2):
                                if pc == 0:
                                    bank_free(2 * gr + j, R_DN + i)
                                kts = (8, 8, 6)[pc]
                                for k in range(kts):
                                    w = (slice(None), k, slice(j * P, (j + 1) * P))
                                    ins = passes(pj[2 * gr + j][:], w_hi[n6 % 2][w], w_lo[n6 % 2][w],
                                                 hid_hi[:, 8 * pc + k, :], hid_lo[:, 8 * pc + k, :],
                                                 pc == 0 and k == 0, pc == 2 and k == kts - 1)
                            ins.then_inc(unit_used, 1)
                    mean_square(("ms", l, "ffn_post"), SQ2, 0, T, SQ_SEEN[l, "ffn_post"])

            eng.wait_ge(sem("route_in"), 48)
            eng.wait_ge(sem("hm_ready"), KT)
            for t in range(2):
                bank = tile(("logit", t))
                for k in range(KT):
                    ins = eng.matmul(bank[:, 0:NE], HM[:, k, t * P:(t + 1) * P], rw[:, k, :],
                                     start=(k == 0), stop=(k == KT - 1))
                filled(ins)
            for i in range(4):
                bank = tile(("h2", i))
                for k in range(4):
                    kt = 4 * (i % 2) + k
                    ins = eng.transpose(bank[:, k * P:(k + 1) * P], HM[:, kt, (i // 2) * P:(i // 2 + 1) * P], ident[:])
                filled(ins)
            eng.wait_ge(sem("sel_ready"), 1)
            bank = tile("rank")
            eng.matmul(bank[:, 0:8], ltri[:], sel[:, 0, :], start=True, stop=True)
            eng.matmul(bank[:, 8:16], ltri[:], sel[:, 1, :], start=True, stop=False)
            eng.matmul(bank[:, 8:16], ones_1[:], sel[:, 0, :], start=False, stop=True)
            eng.matmul(bank[:, 16:24], ones_1[:], sel[:, 0, :], start=True, stop=False)
            filled(eng.matmul(bank[:, 16:24], ones_1[:], sel[:, 1, :], start=False, stop=True))
            eng.wait_ge(sem("one_hot_ready"), 1)
            bank = tile("gslot")
            for j in range(JOBS):
                for t in range(2):
                    ins = eng.matmul(bank[:, j:j + 1], one_hot[:, t, j, :].bitcast(F32), gates[:, t, j:j + 1],
                                     start=(t == 0), stop=(t == 1))
            filled(ins)
            for j in range(JOBS):
                bank = tile(("pT", j))
                for t in range(2):
                    ins = eng.transpose(bank[:, t * P:(t + 1) * P], one_hot[:, t, j, :].bitcast(F32), ident[:])
                filled(ins)
            assert told[0] == MISC_N

            eng.wait_ge(sem("jobs_ready"), 1)
            for b in range(4):
                eng.wait_ge(mi_free[b], MISC_USED[b])
            n_jobs = eng.value_load(jobs[0:1, 0:1], min_val=NE, max_val=JOBS)
            def gather(j, h2, half):
                bank = mi[2 + half]
                for k in range(4):
                    kt = 4 * half + k
                    for t in range(2):
                        ins = eng.matmul(bank[:, k * P:(k + 1) * P], h2[:, t, kt * P:(kt + 1) * P],
                                         one_hot[:, t, bass.ds(j, 1), :].rearrange("p a n -> p (a n)"),
                                         start=(t == 0), stop=(t == 1))
                ins.then_inc(sem("gathered"), 1)

            def scatter(j, r):
                if r >= 2:
                    eng.wait_ge(sem("acc_done"), 4 * j + r + 3)
                for k in range(2):
                    kt = 2 * r + k
                    dst = mi[2 + r % 2][:, k * S:(k + 1) * S]
                    sc = scat[:, bass.ds(j, 1), :].rearrange("p a n -> p (a n)")
                    eng.matmul(dst, ye_hi[:, kt * P:(kt + 1) * P], sc, start=True, stop=False)
                    ins = eng.matmul(dst, ye_lo[:, kt * P:(kt + 1) * P], sc, start=False, stop=True)
                ins.then_inc(sem("scattered"), 1)

            with eng.Fori(0, 1) as j:
                for half in range(2):
                    gather(j, h2_hi, half)
                for half in range(2):
                    eng.wait_ge(sem("xg_hi_done"), half + 1)
                    gather(j, h2_lo, half)
            with eng.Fori(0, n_jobs) as j:
                def down(n, st):
                    eng.wait_ge(lo_dve, DENSE_UNITS + j * JU + n + 1)
                    eng.wait_ge(lo_pool, DENSE_UNITS + j * JU + n + 1)
                    eng.wait_ge(sem("ht_lo_done"), j * STEPS + st + 1)
                    for half in range(2):
                        for t2 in range(2):
                            w = slice(t2 * D + half * 512, t2 * D + half * 512 + 512)
                            ins = passes(pj[2 + half][:], ht_hi[st % 2][:, t2, :], ht_lo[st % 2][:, t2, :],
                                         mw_hi[n % HL_M][:, w], mw_lo[n % HL_M][:, w],
                                         st == 0 and t2 == 0, st == STEPS - 1 and t2 == 1)
                    ins.then_inc(unit_used, 1)

                def turn(st):
                    eng.wait_ge(sem("he_done"), j * STEPS + st + 1)
                    if st >= 2:
                        eng.wait_ge(sem("ht_lo_done"), j * STEPS + st - 1)
                    for t2 in range(2):
                        ins = eng.transpose(mi[st % 2][:, t2 * P:(t2 + 1) * P], he[st % 2][:, t2 * P:(t2 + 1) * P],
                                            ident[:])
                    ins.then_inc(sem("turned"), 1)

                eng.wait_ge(sem("xg_cut"), 2 * j + 2)
                for n, (kind, st) in enumerate(ORDER):
                    if kind == "D":
                        if st == STEPS - 2:
                            for half in range(2):
                                eng.wait_ge(sem("xg_hi_done"), 2 * j + 3 + half)
                                gather(j + 1, h2_lo, half)
                            turn(STEPS - 1)
                        down(n, st)
                        continue
                    eng.wait_ge(lo_dve, DENSE_UNITS + j * JU + n + 1)
                    eng.wait_ge(lo_pool, DENSE_UNITS + j * JU + n + 1)
                    if kind == "A" and st >= 2:
                        eng.wait_ge(sem("he_done"), j * STEPS + st - 1)
                    for k in range(4):
                        kt = k + (0 if kind == "A" else 4)
                        ins = passes(pj[st % 2][:], xg_hi[:, kt, :], xg_lo[:, kt, :],
                                     mw_hi[n % HL_M][:, k * 512:(k + 1) * 512],
                                     mw_lo[n % HL_M][:, k * 512:(k + 1) * 512],
                                     kt == 0, kt == KT - 1)
                    ins.then_inc(unit_used, 1)
                    if kind == "B" and st >= 1:
                        turn(st - 1)
                    if kind == "B" and st <= 1:
                        if st == 0:
                            eng.wait_ge(sem("ye_lo_done"), 2 * j + 2)
                        scatter(j, 2 * st)
                        scatter(j, 2 * st + 1)
                    if (kind, st) == ("B", STEPS - 1):
                        eng.wait_ge(sem("acc_done"), 4 * j + 8)
                        for half in range(2):
                            gather(j + 1, h2_hi, half)
            eng.wait_ge(sem("ye_lo_done"), n_jobs * 2 + 2)
            eng.wait_ge(sem("xg_cut"), n_jobs * 2 + 2)
            for r in range(4):
                scatter(n_jobs, r)

            for k in range(KT):
                eng.wait_ge(sem("squared"), 56 + k + 1)
                ins = eng.matmul(pj[0][:, 0:S], ones_d[:], SQM[:, k, :], start=(k == 0), stop=(k == KT - 1))
            ins.then_inc(sem("last_ms"), 1)
            eng.wait_ge(sem("r_ready"), 4 * KT)
            for i in range(4):
                for k in range(4):
                    kt = 4 * (i % 2) + k
                    t = i // 2
                    ins = eng.transpose(mi[i][:, k * P:(k + 1) * P], R[:, kt, S + t * P:S + (t + 1) * P], ident[:])
                ins.then_inc(sem("last_turned"), 1)

        @block.scalar
        def _(eng):
            act = Steps(eng, sem("act_steps"))

            def copy(dst, src, func=ACT.Copy, **kw):
                return eng.activation(dst, src, func, **kw)

            def cut_hi(pair, p):
                if isinstance(pair, int) and 2 * pair + p >= DENSE_UNITS:
                    return
                eng.wait_ge(raw_in[p], 32 * (pair + 1))
                if not isinstance(pair, int) or pair > 0:
                    eng.wait_ge(unit_used, 2 * pair + p - 1)
                copy(w_hi[p][:], raw[p][:]).then_inc(hi_done, 1)

            def used(n):
                eng.wait_ge(unit_used, n + 1)

            eng.wait_ge(sem("c_in"), 32)
            copy(csil[:].rearrange("p k s -> p s k"), craw[:], ACT.Silu).then_inc(sem("csil_done"), 1)
            eng.wait_ge(sem("lb_shifted"), 1)
            copy(lbp[:, 2:4, :], lbp[:, 0:2, :], ACT.Exp).then_inc(sem("lb_exp"), 1)
            eng.wait_ge(sem("lb_sum"), 1)
            copy(lbp[:, 5, :], lbp[:, 4, :], ACT.Ln).then_inc(sem("lb_ln"), 1)

            def squares(k, n, c0, ready):
                if ready is None:
                    bank, free, full, before = mi_of(("xT", k))
                    eng.wait_ge(free, before + 1)
                else:
                    eng.wait_ge(sem("r_ready"), ready + k)
                copy(SQ[:, k, c0:c0 + n], R[:, k, c0:c0 + n], ACT.Square).then_inc(sem("squared"), 1)

            def inverse_root(name, norm, n):
                bank, free, full, before = mi_of(name)
                eng.wait_ge(mi_full, full)
                if norm > 1:
                    eng.wait_ge(sem("rstd_used"), norm - 1)
                copy(rstd[:, 0:n], bank[:, 0:n], ACT.Ln, bias=eps_t[:]).then_inc(free, 1)
                eng.wait_ge(free, before + 1)
                copy(rstd[:, 0:n], rstd[:, 0:n], ACT.Exp, scale=-0.5).then_inc(sem("rstd_ready"), 1)

            def cut_h_hi(done, c0, n):
                for k in range(KT):
                    eng.wait_ge(sem("h_ready"), done + k + 1)
                    copy(h_hi[:, k, c0:c0 + n], HF[:, k, c0:c0 + n]).then_inc(sem("h_hi_done"), 1)

            def evac(pair, dst, n, func):
                for p in range(2):
                    used(2 * pair + p)
                    for b in (2 * p, 2 * p + 1):
                        x = dst(b)
                        src = pj[b][:, 0:n]
                        if len(x.shape) == 3:
                            src = src.rearrange("p (s t) -> p s t", t=S)
                        copy(x, src, func).then_inc(pj_free[b], 1)
                    cut_hi(pair + 1, p)

            def forget_gates(l, dirs):
                for d in dirs:
                    turn = 2 * l + d + 1
                    if turn > 1:
                        eng.wait_ge(sem("gate_done"), turn - 1)
                        eng.wait_ge(sem("keys_done"), turn - 1)
                    eng.wait_ge(pj_free[3], R_IN[l] + 1 + d)
                    act.step(copy(gE[:], lf[:, d], ACT.Abs))
                    act.step(copy(gE[:], gE[:], ACT.Exp, scale=-1.0))
                    copy(gL[:], gE[:], ACT.Ln, bias=1.0).then_inc(sem("gate_l1"), 1)
                    eng.wait_ge(sem("gate_e"), turn)
                    if l == 0:
                        copy(kk[:, d], gE[:], ACT.Exp, scale=-1.0).then_inc(sem("keys_done"), 1)
                        continue
                    for hd in range(HEADS):
                        ins = copy(kk[:, d, :, hd, :], gE[:, :, hd, :], ACT.Exp, scale=-1.0,
                                   bias=lbp[:, 0, d * 4 + hd:d * 4 + hd + 1])
                        ins.then_inc(*((sem("keys_done"), 1) if hd == HEADS - 1 else (sem("key_heads"), 1)))
                    eng.wait_ge(sem("gate_diff"), d + 1)
                    act.step(copy(gL[:], gE[:], ACT.Abs))
                    act.step(copy(gL[:], gL[:], ACT.Exp, scale=-1.0))
                    copy(gL[:], gL[:], ACT.Ln, bias=1.0).then_inc(sem("gate_l2"), 1)

            last_use = [[], []]

            def decays(l, s, d):
                for li, h in enumerate(LEVELS + [S]):
                    if li < 8 and not FULL[l, s]:
                        continue
                    i = li % 2
                    for w in last_use[i]:
                        eng.wait_ge(*w)
                    eng.wait_ge(sem("ab_ready"), N_EXP[l, s, d, li])
                    if li == 8:
                        if s == 1:
                            copy(QE[0][:], cA[:], ACT.Exp).then_inc(sem("decayed"), 1)
                            last_use[0] = [(sem("q_ready"), N_Q[l, s, d, 8])]
                        else:
                            copy(KE[0][:], cB[:], ACT.Exp).then_inc(sem("decayed"), 1)
                            last_use[0] = [(mi_full, MISC[("kT", l, d, 1)][1])]
                        continue
                    tq, ts = (1, 0) if d == 0 else (0, 1)
                    view = lambda x: x[:].rearrange("p e (b two h) -> p (e b) two h", two=2, h=h)
                    act.mark(copy(view(QE[i])[:, :, tq, :], view(cA)[:, :, tq, :], ACT.Exp))
                    copy(view(KE[i])[:, :, ts, :], view(cB)[:, :, ts, :], ACT.Exp).then_inc(sem("decayed"), 1)
                    last_use[i] = [(mi_full, MISC[("att", l, s, d, li, 1 if h < P else 0)][1])]

            def copy_out(name, dst):
                bank, free, full, before = mi_of(name)
                eng.wait_ge(mi_full, full)
                copy(dst, bank[:].rearrange("p (e n) -> p e n", e=HEADS)).then_inc(free, 1)

            def halves(x, i):
                return x[:, 2 * i:2 * i + 2, :].rearrange("p e t -> p (e t)")

            def head_norm(l, s):
                for i in range(2):
                    bank, free, full, before = mi_of(("o", l, s, i))
                    eng.wait_ge(mi_full, full)
                    copy(halves(cA, i), bank[:], ACT.Square).then_inc(sem("o_squared"), 1)
                for i in range(2):
                    bank, free, full, before = mi_of(("oms", l, s, i))
                    eng.wait_ge(mi_full, full)
                    copy(halves(cB, i), bank[:], ACT.Ln, bias=eps_t[:]).then_inc(free, 1)
                    eng.wait_ge(free, before + 1)
                    copy(halves(cB, i), halves(cB, i), ACT.Exp, scale=-0.5).then_inc(sem("o_rstd"), 1)

            def residual_norm(l, name, norm, ready):
                c0, n = (0, T) if name == "mix_pre" else (C0[l], NT[l])
                for k in range(KT):
                    squares(k, n, c0, ready)
                if norm == 1:
                    for p in range(2):
                        cut_hi(0, p)
                inverse_root(("ms", l, name), norm, n)

            def evac_out(pair, first_kt, y, sq, c0, n):
                for p in range(2):
                    used(2 * pair + p)
                    for j in range(2):
                        b, kt = 2 * p + j, first_kt + 2 * p + j
                        copy(sq[:, kt, c0:c0 + n], pj[b][:, 0:n], ACT.Square).then_inc(sem("squared"), 1)
                        copy(y[:, kt, c0:c0 + n], pj[b][:, 0:n]).then_inc(pj_free[b], 1)
                    cut_hi(pair + 1, p)

            eng.wait_ge(sem("ones_set"), 3)
            for l in range(2):
                c0, n = C0[l], NT[l]
                up = U_IN[l] // 2
                residual_norm(l, "mix_pre", 4 * l + 1, None if l == 0 else KT + 1)
                cut_h_hi(2 * KT * l, 0, T)
                if l == 1:
                    eng.wait_ge(sem("lb_ready"), 1)
                for d in range(2):
                    evac(up + d, lambda b: lf[:, d, :, b, :], T, ACT.Copy)
                    forget_gates(l, [d])
                evac(up + 2, lambda b: u[:, b, c0:c0 + n], n, ACT.Copy)
                used(2 * (up + 3))
                cut_hi(up + 4, 0)
                used(2 * (up + 3) + 1)
                for t in range(4):
                    copy(v[:, t, :], pj[t][:]).then_inc(pj_free[t], 1)
                cut_hi(up + 4, 1)
                evac(up + 4, lambda b: g[:, b, c0:c0 + n], n, ACT.Silu)
                evac(up + 5, lambda b: q[:, c0 // S:2, b, :], n, ACT.Silu)
                last_use[0] = last_use[1] = [(sem("gate_done"), 2 * l + 2), (sem("keys_done"), 2 * l + 2)]
                for s in range(2):
                    if FULL[l, s]:
                        last_use[1] = [(mi_full, MISC[("diag", l, s, 1)][1])]
                        last_use[0] = last_use[0] + [(sem("diag_q"), 1 + s + l), (sem("diag_k"), 1 + s + l)]
                    for d in range(2):
                        decays(l, s, d)
                        if s == 0:
                            for t in range(2):
                                copy_out(("kT", l, d, t), kept_keys(d)[:, t])
                            copy_out(("st", l, d), state[:, d])
                    if FULL[l, s]:
                        head_norm(l, s)
                for k in range(2):
                    eng.wait_ge(pj_free[k], R_IN[l] + 6)
                for i in range(4):
                    for p in range(2):
                        used(U_IN[l] + 12 + 2 * i + p)
                        for j in range(2):
                            b = 2 * p + j
                            if (l, i, p) != (0, 0, 0):
                                eng.wait_ge(sem(f"spilled{j}"), 16 * (8 * l + 2 * i + p))
                            copy(gate_st[j][:, 0:n], pj[b][:, 0:n], ACT.Sigmoid).then_inc(pj_free[b], 1)
                            eng.wait_ge(pj_free[b], R_IN[l] + 7 + i)
                            eng.dma_start(spill[4 * i + b, :, 0:n],
                                          gate_st[j][:, 0:n]).then_inc(sem(f"spilled{j}"), 16)
                        cut_hi(up + 7 + i, p)
                used(U_IN[l] + N_IN - 1)
                eng.wait_ge(sem("y_rec"), (2, 3)[l])
                for src, hi in ((g, yr_hi), (u, yp_hi)):
                    for i in range(2):
                        copy(hi[:, 2 * i:2 * i + 2, c0:c0 + n], src[:, 2 * i:2 * i + 2, c0:c0 + n])\
                            .then_inc(sem("branch_hi"), 1)
                for b in range(N_BR):
                    for j in range(2):
                        eng.wait_ge(sem("m_ready"), 8 * l + 2 * b + j + 1)
                        copy(m_hi[:, 2 * b + j, c0:c0 + n], mt[2 * j][:, 0:n]).then_inc(sem("m_hi_done"), 1)
                    cut_hi((U_BR[l] + b) // 2 + 1, b % 2)
                for i in range(2):
                    evac_out(U_OUT[l] // 2 + i, 4 * i, Y, SQ, c0, n)
                inverse_root(("ms", l, "mix_post"), 4 * l + 2, n)
                residual_norm(l, "ffn_pre", 4 * l + 3, 2 * KT * l + 1)
                if l == 0:
                    cut_h_hi(KT, 0, T)
                    with eng.Fori(0, N_GU // 2) as i:
                        pair = U_GU // 2 + i
                        used(2 * pair)
                        for j in range(2):
                            eng.wait_ge(pj_free[2 + j], R_GU + i)
                            copy(sg[:, j, :], pj[j][:], ACT.Silu).then_inc(pj_free[j], 1)
                        cut_hi(pair + 1, 0)
                        cut_hi(pair + 1, 1)
                        for j in range(2):
                            eng.wait_ge(pj_free[2 + j], R_GU + i + 1)
                            copy(hid_hi[:, bass.ds(2 * i + j, 1), :].rearrange("p a n -> p (a n)"), hf[:, j, :])\
                                .then_inc(sem("hid_hi_done"), 1)
                    for gr in range(4):
                        for pc in range(3):
                            used(U_DN + 3 * gr + pc)
                            if pc == 2:
                                for j in range(2):
                                    b, kt = 2 * (gr % 2) + j, 2 * gr + j
                                    copy(SQ2[:, kt, :], pj[b][:], ACT.Square).then_inc(sem("squared"), 1)
                                    copy(Y2[:, kt, :], pj[b][:]).then_inc(pj_free[b], 1)
                            nxt = U_DN + 3 * gr + pc + 2
                            cut_hi(nxt // 2, nxt % 2)
                    inverse_root(("ms", l, "ffn_post"), 4, T)

            eng.wait_ge(sem("top_diff"), 1)
            copy(tmp1[:, 2:4], tmp1[:, 0:2], ACT.Exp).then_inc(sem("top_exp"), 1)
            for i in range(4):
                bank, free, full, before = mi_of(("h2", i))
                eng.wait_ge(mi_full, full)
                copy(h2_hi[:, i // 2, (i % 2) * 512:(i % 2 + 1) * 512], bank[:]).then_inc(sem("h2_hi_done"), 1)
            copy(scat[:, 0, :], HM[:, 0, :], scale=0.0).then_inc(sem("scat_first"), 1)
            for j in range(JOBS):
                bank, free, full, before = mi_of(("pT", j))
                eng.wait_ge(mi_full, full)
                copy(scat[:, j + 1, :], bank[:, 0:S]).then_inc(free, 1)
            eng.wait_ge(sem("jobs_ready"), 1)
            n_jobs = eng.value_load(jobs[0:1, 0:1], min_val=NE, max_val=JOBS)

            def gathered_hi(j):
                for half in range(2):
                    eng.wait_ge(sem("gathered"), 4 * j + half + 1)
                    copy(xg_hi[:, 4 * half:4 * half + 4, :].rearrange("p k n -> p (k n)"), mi[2 + half][:])\
                        .then_inc(sem("xg_hi_done"), 1)

            def scaled_hi(j):
                for half in range(2):
                    copy(ye_hi[:, half * 512:(half + 1) * 512], pj[2 + half][:],
                         scale=gslot[:, bass.ds(j, 1)]).then_inc(sem("ye_hi_done"), 1)

            gathered_hi(0)
            with eng.Fori(0, n_jobs) as j:
                def cut_job_hi(n):
                    eng.wait_ge(rawm_in[n % RAW_M], (JU // RAW_M * 32) * j + 32 * (n // RAW_M + 1))
                    eng.wait_ge(unit_used, DENSE_UNITS + j * JU + n - HL_M + 1)
                    copy(mw_hi[n % HL_M][:], raw_m[n % RAW_M][:]).then_inc(hi_done, 1)

                def turned_hi(st):
                    eng.wait_ge(sem("turned"), j * STEPS + st + 1)
                    copy(ht_hi[st % 2][:].rearrange("p a n -> p (a n)"), mi[st % 2][:, 0:256])\
                        .then_inc(sem("ht_hi_done"), 1)

                for n in range(HL_M):
                    cut_job_hi(n)
                scaled_hi(j)
                for n, (kind, st) in enumerate(ORDER):
                    if kind == "B":
                        eng.wait_ge(unit_used, DENSE_UNITS + j * JU + n + 1)
                        if st >= 2:
                            eng.wait_ge(sem("he_done"), j * STEPS + st - 1)
                        copy(sge[st % 2][:], pj[st % 2][:, 0:256], ACT.Silu).then_inc(sem("sge_done"), 1)
                    if n + HL_M < JU:
                        cut_job_hi(n + HL_M)
                    if kind == "B" and st >= 1:
                        turned_hi(st - 1)
                    if (kind, st) == ("B", STEPS - 1):
                        gathered_hi(j + 1)
                    if (kind, st) == ("D", STEPS - 3):
                        turned_hi(STEPS - 1)
            eng.wait_ge(unit_used, n_jobs * JU + DENSE_UNITS)
            scaled_hi(n_jobs)
            eng.wait_ge(sem("acc_done"), n_jobs * 4 + 8)
            for k in range(KT):
                copy(SQM[:, k, :], acc[:, k, :], ACT.Square).then_inc(sem("squared"), 1)
            eng.wait_ge(sem("last_ms"), 1)
            act.step(copy(rstd[:, 0:S], pj[0][:, 0:S], ACT.Ln, bias=eps_t[:]))
            copy(rstd[:, 0:S], rstd[:, 0:S], ACT.Exp, scale=-0.5).then_inc(sem("rstd_ready"), 1)

        @block.vector
        def _(eng):
            dve = Steps(eng, sem("dve_steps"))
            tt, ts_, stt = eng.tensor_tensor, eng.tensor_scalar, eng.scalar_tensor_tensor

            def cut_lo(pair, p):
                if isinstance(pair, int) and 2 * pair + p >= DENSE_UNITS:
                    return
                eng.wait_ge(hi_done, 2 * pair + p + 1)
                k = slice(0, VK)
                tt(w_lo[p][:, k, :], raw[p][:, k, :], w_hi[p][:, k, :], ALU.subtract).then_inc(lo_dve, 1)

            def full_tile(name):
                bank, free, full, before = mi_of(name)
                eng.wait_ge(mi_full, full)
                return bank, free

            eng.memset(ones_d[:], 1.0 / D).then_inc(sem("ones_set"), 1)
            eng.memset(ones_h[:], 1.0 / P).then_inc(sem("ones_set"), 1)
            eng.memset(eps_t[:], EPS).then_inc(sem("ones_set"), 1)
            for k in range(KT):
                bank, free = full_tile(("xT", k))
                eng.tensor_copy(R[:, k, :], bank[:]).then_inc(free, 1)
            bank, free = full_tile("prmA")
            eng.tensor_copy(adab[:], bank[:, 0:96]).then_inc(free, 1)
            bank, free = full_tile("prmB")
            eng.tensor_copy(prm[:], bank[:, 0:96]).then_inc(free, 1)
            eng.wait_ge(free, MISC["prmB"][2] + 1)
            eng.wait_ge(sem("consts_in"), 32)
            eng.tensor_copy(masks[:], masks_f[:]).then_inc(sem("masks_set"), 1)
            dve.step(tt(lbp[:, 4, :], prm[:, 64:72], prm[:, 72:80], ALU.max))
            dve.mark(tt(lbp[:, 0, :], prm[:, 64:72], lbp[:, 4, :], ALU.subtract))
            tt(lbp[:, 1, :], prm[:, 72:80], lbp[:, 4, :], ALU.subtract).then_inc(sem("lb_shifted"), 1)
            eng.wait_ge(sem("lb_exp"), 1)
            tt(lbp[:, 4, :], lbp[:, 2, :], lbp[:, 3, :], ALU.add).then_inc(sem("lb_sum"), 1)
            eng.wait_ge(sem("lb_ln"), 1)
            dve.mark(tt(lbp[:, 0, :], lbp[:, 0, :], lbp[:, 5, :], ALU.subtract))
            tt(lbp[:, 1, :], lbp[:, 1, :], lbp[:, 5, :], ALU.subtract).then_inc(sem("lb_ready"), 1)
            b0 = MISC[("ada", 0)][0]
            flat = mod[:].rearrange("p l c s -> p (l c s)")
            with eng.Fori(0, ADA_UNITS // 4) as i:
                for s in range(4):
                    b = (b0 + s) % 4
                    eng.wait_ge(mi_full, MISC[("ada", s)][1] + 4 * i)
                    eng.tensor_copy(flat[:, bass.ds(16 * i + 4 * s, 4)], mi[b][:, 0:4]).then_inc(mi_free[b], 1)
            for s in range(4):
                eng.wait_ge(mi_free[(b0 + s) % 4], MISC[("ada", s)][2] + ADA_UNITS // 4)
            bias = adab[:].rearrange("p (l c s) -> p l c s", l=2, s=1).to_broadcast([P, 2, 48, 2])
            for l in range(2):
                dve.mark(tt(mod[:, l], mod[:, l], bias[:, l], ALU.add))
            dve.sync()
            for l in range(2):
                for chunk, row, plus in ((1, 0, 1.0), (4, 32, 1.0), (2, 16, 0.0), (5, 48, 0.0)):
                    m = mod[:, l, 8 * chunk:8 * chunk + 8, :]
                    w = prm[:, row + 8 * l:row + 8 * l + 8].rearrange("p (c s) -> p c s", s=1).to_broadcast([P, 8, 2])
                    dve.mark(stt(m, m, plus, w, ALU.add, ALU.mult))
            dve.sync()

            def column(l, chunk, k, s):
                return mod[:, l, 8 * chunk + k, s:s + 1]

            def streams(l, name):
                return (0, 1) if l == 0 or name == "mix_pre" else (1,)

            def modulate(l, name, norm, dst, d0, signal):
                chunk = 0 if name == "mix_pre" else 3
                eng.wait_ge(sem("rstd_ready"), norm)
                sts = streams(l, name)
                c0, n = sts[0] * S, len(sts) * S
                for k in range(KT):
                    ins = tt(dst[:, k, c0 - d0:c0 - d0 + n], R[:, k, c0:c0 + n], rstd[:, 0:n], ALU.mult)
                    ins.then_inc(*((sem("rstd_used"), 1) if k == KT - 1 else (dve.sem, 1)))
                    dve.k += k < KT - 1
                eng.wait_ge(sem("rstd_used"), norm)
                for k in range(KT):
                    for s in sts:
                        x = dst[:, k, s * S - d0:(s + 1) * S - d0]
                        ins = ts_(x, x, column(l, chunk + 1, k, s), column(l, chunk, k, s), ALU.mult, ALU.add)
                        ins.then_inc(*((signal, 1) if s == sts[-1] else (dve.sem, 1)))
                        dve.k += s != sts[-1]

            def cut_h_lo(done, c0, n):
                for k in range(KT):
                    eng.wait_ge(sem("h_hi_done"), done + k + 1)
                    tt(h_lo[:, k, c0:c0 + n], HF[:, k, c0:c0 + n], h_hi[:, k, c0:c0 + n], ALU.subtract)\
                        .then_inc(sem("h_cut"), 1)

            def add_branch(l, chunk, norm, y, c0, n, y0=0):
                eng.wait_ge(sem("rstd_ready"), norm)
                for k in range(KT):
                    yk = y[:, k, c0 - y0:c0 - y0 + n]
                    ins = tt(yk, yk, rstd[:, 0:n], ALU.mult)
                    ins.then_inc(*((sem("rstd_used"), 1) if k == KT - 1 else (dve.sem, 1)))
                    dve.k += k < KT - 1
                eng.wait_ge(sem("rstd_used"), norm)
                for k in range(KT):
                    for s in ((0, 1) if n == T else (1,)):
                        r = R[:, k, s * S:(s + 1) * S]
                        ins = stt(r, y[:, k, s * S - y0:(s + 1) * S - y0], column(l, chunk, k, s), r, ALU.mult, ALU.add)
                        ins.then_inc(*((sem("r_ready"), 1) if s == 1 else (dve.sem, 1)))
                        dve.k += s != 1

            def flat(x):
                return x.rearrange("p s e t -> p (s e t)")

            def forget_gates(l, dirs):
                for d in dirs:
                    turn = 2 * l + d + 1
                    z = flat(lf[:, d])
                    eng.wait_ge(sem("gate_l1"), turn)
                    stt(flat(gE[:]), z, 0.0, flat(gL[:]), ALU.max, ALU.add).then_inc(sem("gate_e"), 1)
                    eng.wait_ge(sem("gate_e"), turn)
                    ins = stt(z, z, 0.0, flat(gL[:]), ALU.min, ALU.subtract)
                    if l == 0:
                        ins.then_inc(sem("gate_done"), 1)
                        continue
                    dve.step(ins)
                    for hd in range(HEADS):
                        x = lf[:, d, :, hd, :]
                        dve.mark(ts_(x, x, lbp[:, 0, d * 4 + hd:d * 4 + hd + 1], None, ALU.add))
                    dve.sync()
                    eng.wait_ge(sem("keys_done"), turn)
                    for hd in range(HEADS):
                        ins = ts_(gE[:, :, hd, :], lf[:, d, :, hd, :], lbp[:, 1, d * 4 + hd:d * 4 + hd + 1],
                                  None, ALU.subtract)
                        if hd < HEADS - 1:
                            dve.mark(ins)
                    ins.then_inc(sem("gate_diff"), 1)
                    eng.wait_ge(sem("gate_diff"), d + 1)
                    for hd in range(HEADS):
                        x = lf[:, d, :, hd, :]
                        dve.mark(ts_(x, x, lbp[:, 1, d * 4 + hd:d * 4 + hd + 1], None, ALU.max))
                    dve.sync()
                    eng.wait_ge(sem("gate_l2"), d + 1)
                    tt(z, z, flat(gL[:]), ALU.add).then_inc(sem("gate_done"), 1)

            taken = [None, None]

            def take(name, t, dst, mask=None):
                bank, free = full_tile(name)
                if taken[t]:
                    eng.wait_ge(*taken[t])
                src = bank[:].rearrange("p (e n) -> p e n", e=HEADS)
                if mask is None:
                    eng.tensor_copy(dst, src).then_inc(free, 1)
                else:
                    eng.copy_predicated(dst, mask, src).then_inc(free, 1)
                taken[t] = (free, MISC[name][2] + 1)

            def take_products(l, s, d, li):
                if LEVELS[li] == P:
                    st, qt = (0, 1) if d == 0 else (1, 0)
                    take(("att", l, s, d, li, 0), st, att[:, st, :, qt * P:(qt + 1) * P])
                    return
                mask = masks[:, 7 * d + li:7 * d + li + 1, :].to_broadcast([P, HEADS, P])
                for t in range(2):
                    take(("att", l, s, d, li, t), t, att[:, t, :, t * P:(t + 1) * P], mask)

            def halves_of(x, h):
                return x.rearrange("p e (b two h) -> p (e b) two h", two=2, h=h)

            def scan(l, s, d):
                n = SCANS.index((l, s, d))
                if n:
                    eng.wait_ge(sem("decayed"), N_EXP[SCANS[n - 1] + (8,)])
                dve.mark(eng.tensor_copy(cA[:], lf[:, d, s]))
                ins = eng.memset(cB[:], 0.0)
                if FULL[l, s]:
                    ins.then_inc(sem("ab_ready"), 1)
                    eng.wait_ge(sem("ab_ready"), N_EXP[l, s, d, 0])
                else:
                    dve.step(ins)
                tq, tk = (1, 0) if d == 0 else (0, 1)
                for li, h in enumerate(LEVELS):
                    if FULL[l, s]:
                        eng.wait_ge(sem("decayed"), N_EXP[l, s, d, li])
                        x = halves_of(QE[li % 2][:], h)[:, :, tq, :]
                        stt(x, x, HS, halves_of(q[:, s], h)[:, :, tq, :], ALU.mult, ALU.mult)\
                            .then_inc(sem("q_ready"), 1)
                    a_, b_ = halves_of(cA[:], h), halves_of(cB[:], h)
                    edge = h - 1 if d == 0 else 0
                    half = [P, a_.shape[1], h]
                    dve.step(tt(b_[:, :, tk, :], b_[:, :, tk, :], a_[:, :, tq, edge:edge + 1].to_broadcast(half),
                                ALU.add))
                    ins = tt(a_[:, :, tq, :], a_[:, :, tq, :], a_[:, :, tk, edge:edge + 1].to_broadcast(half), ALU.add)
                    if FULL[l, s] or li == 7:
                        ins.then_inc(sem("ab_ready"), 1)
                        nxt = N_EXP[l, s, d, li + 1]
                        eng.wait_ge(sem("ab_ready"), nxt)
                    else:
                        dve.step(ins)
                    if FULL[l, s] and li == 0 and d == 0:
                        for t in range(2):
                            take(("diag", l, s, t), t, att[:, t, :, t * P:(t + 1) * P])
                    if FULL[l, s] and li >= 1:
                        take_products(l, s, d, li - 1)
                if FULL[l, s]:
                    take_products(l, s, d, 7)
                if s == 1:
                    eng.wait_ge(sem("decayed"), N_EXP[l, s, d, 8])
                    stt(lf[:, d, 1], QE[0][:], HS, q[:, 1], ALU.mult, ALU.mult).then_inc(sem("q_ready"), 1)

            def head_norm(l, s, turn):
                for i in range(2):
                    bank, free, full, before = mi_of(("o", l, s, i))
                    eng.wait_ge(sem("o_rstd"), 2 * turn + i + 1)
                    x = slice(2 * i, 2 * i + 2)
                    tt(cA[:, x, :], bank[:].rearrange("p (e n) -> p e n", e=2), cB[:, x, :], ALU.mult).then_inc(free, 1)
                    eng.wait_ge(free, before + 1)
                for hd in range(HEADS):
                    y = g[:, hd, s * S:(s + 1) * S]
                    ins = stt(y, cA[:, hd, :], prm[:, 80 + 4 * l + hd:81 + 4 * l + hd], y, ALU.mult, ALU.mult)
                    if hd < HEADS - 1:
                        dve.mark(ins)
                ins.then_inc(sem("y_rec"), 1)

            def cut_pairs(first, last):
                with eng.Fori(first, last) as i:
                    for p in range(2):
                        cut_lo(i, p)

            for p in range(2):
                cut_lo(0, p)
            turn = 0
            for l in range(2):
                c0, n = C0[l], NT[l]
                up = U_IN[l] // 2
                modulate(l, "mix_pre", 4 * l + 1, HF, 0, sem("h_ready"))
                cut_h_lo(2 * KT * l, 0, T)
                for d in range(2):
                    cut_pairs(up + 1 + d, up + 2 + d)
                    forget_gates(l, [d])
                cut_pairs(up + 3, up + 7)
                eng.wait_ge(pj_free[3], R_IN[l] + 6)
                for gi in range(4):
                    bank, free = full_tile(("pool", l, gi))
                    ts_(u[:, gi, c0:c0 + n], bank[:, 0:n], prm[:, 88 + 4 * l + gi:89 + 4 * l + gi], None, ALU.mult)\
                        .then_inc(free, 1)
                if l == 0:
                    eng.wait_ge(sem("masks_set"), 1)
                eng.wait_ge(sem("keys_done"), 2 * l + 2)
                eng.wait_ge(sem("gate_done"), 2 * l + 2)
                for s in range(2):
                    if FULL[l, s]:
                        if (l, s) == (0, 1):
                            eng.wait_ge(mi_full, MISC[("att", 0, 0, 1, 7, 0)][1])
                        if (l, s) != (0, 1):
                            dve.mark(eng.memset(QE[0][:], 0.0))
                        ts_(QE[1][:], q[:, s], HS, None, ALU.mult).then_inc(sem("diag_q"), 1)
                    for d in range(2):
                        scan(l, s, d)
                    if FULL[l, s]:
                        head_norm(l, s, turn)
                        eng.wait_ge(sem("y_rec"), turn + 1)
                        turn += 1
                cut_pairs(up + 7, up + 11)
                for i, (src, hi, lo) in enumerate(((g, yr_hi, yr_lo), (u, yp_hi, yp_lo))):
                    for j in range(2):
                        eng.wait_ge(sem("branch_hi"), 4 * l + 2 * i + j + 1)
                        x = (slice(None), slice(2 * j, 2 * j + 2), slice(c0, c0 + n))
                        tt(lo[x], src[x], hi[x], ALU.subtract).then_inc(sem("branches_cut"), 1)
                for b in range(N_BR):
                    eng.wait_ge(unit_used, U_BR[l] + b + 1)
                    eng.wait_ge(sem(f"gates_in{b % 2}"), 32 * (2 * l + b // 2 + 1))
                    if b:
                        eng.wait_ge(sem("m_cut"), 8 * l + 2 * b)
                    for j in range(2):
                        for i in range(2):
                            tt(mt[2 * j + i][:, 0:n], sgate[b % 2][:, i, j, 0:n], pj[2 * i + j][:, 0:n], ALU.mult)\
                                .then_inc(pj_free[2 * i + j], 1)
                        for i in range(2):
                            eng.wait_ge(pj_free[2 * i + j], R_BR[l] + b + 1)
                        tt(mt[2 * j][:, 0:n], mt[2 * j][:, 0:n], mt[2 * j + 1][:, 0:n], ALU.add)\
                            .then_inc(sem("m_ready"), 1)
                    for j in range(2):
                        kt = 2 * b + j
                        eng.wait_ge(sem("m_hi_done"), 8 * l + kt + 1)
                        tt(m_lo[:, kt, c0:c0 + n], mt[2 * j][:, 0:n], m_hi[:, kt, c0:c0 + n], ALU.subtract)\
                            .then_inc(sem("m_cut"), 1)
                    cut_lo((U_BR[l] + b) // 2 + 1, b % 2)
                for i in range(N_OUT // 2):
                    for p in range(2):
                        cut_lo(U_OUT[l] // 2 + i + 1, p)
                add_branch(l, 2, 4 * l + 2, Y, c0, n)
                if l == 1:
                    modulate(1, "ffn_pre", 7, HM, S, sem("hm_ready"))
                    continue
                modulate(0, "ffn_pre", 3, HF, 0, sem("h_ready"))
                cut_h_lo(KT, 0, T)
                with eng.Fori(0, N_GU // 2) as i:
                    pair = U_GU // 2 + i
                    cut_lo(pair + 1, 0)
                    eng.wait_ge(unit_used, 2 * pair + 2)
                    eng.wait_ge(lo_dve, 2 * pair + 3)
                    for j in range(2):
                        eng.wait_ge(pj_free[j], R_GU + i + 1)
                        tt(hf[:, j, :], sg[:, j, :], pj[2 + j][:], ALU.mult).then_inc(pj_free[2 + j], 1)
                    cut_lo(pair + 1, 1)
                    for j in range(2):
                        eng.wait_ge(sem("hid_hi_done"), 2 * i + j + 1)
                        kt = bass.ds(2 * i + j, 1)
                        tt(hid_lo[:, kt, :], hf[:, j:j + 1, :], hid_hi[:, kt, :], ALU.subtract)\
                            .then_inc(sem("hid_cut"), 1)
                cut_pairs(U_DN // 2 + 1, U_DN // 2 + 7)
                add_branch(0, 5, 4, Y2, 0, T)

            dve.mark(eng.memset(ones_1[:], 1.0))
            dve.mark(eng.memset(gslot[:, 0:1], 0.0))
            dve.step(eng.memset(keys[:], -1.0))
            for t in range(2):
                bank, free = full_tile(("logit", t))
                eng.tensor_copy(lg[:, t, :], bank[:, 0:NE]).then_inc(free, 1)
                eng.wait_ge(free, MISC[("logit", t)][2] + 1)
                dve.step(eng.max(top_v[:, t, :], lg[:, t, :]))
                dve.step(eng.max_index(top_i[:, t, :], top_v[:, t, :], lg[:, t, :]))
            dve.step(eng.tensor_copy(top_f[:], top_i[:]))
            eng.wait_ge(sem("route_in"), 48)
            for t in range(2):
                for k in range(2):
                    dve.mark(ts_(tmp8[:, 2 * t + k, :], iota[:, 0:NE], top_f[:, t, k:k + 1], None, ALU.is_equal))
            dve.sync()
            tt(tmp1[:, 0:2].rearrange("p (t a) -> p t a", a=1), top_v[:, :, 1:2], top_v[:, :, 0:1], ALU.subtract)\
                .then_inc(sem("top_diff"), 1)
            for t in range(2):
                ins = tt(sel[:, t, :], tmp8[:, 2 * t, :], tmp8[:, 2 * t + 1, :], ALU.add)
                ins.then_inc(*((sem("sel_ready"), 1) if t else (dve.sem, 1)))
                dve.k += 1 - t
            eng.wait_ge(sem("top_exp"), 1)
            dve.step(ts_(tmp1[:, 4:6], tmp1[:, 2:4], 1.0, None, ALU.add))
            dve.step(eng.reciprocal(tmp1[:, 4:6], tmp1[:, 4:6]))
            dve.step(tt(tmp1[:, 6:8], tmp1[:, 2:4], tmp1[:, 4:6], ALU.mult))
            for t in range(2):
                dve.mark(ts_(gates[:, t, 0:NE], tmp8[:, 2 * t, :], tmp1[:, 4 + t:5 + t], None, ALU.mult))
            dve.sync()
            for t in range(2):
                dve.mark(stt(gates[:, t, 0:NE], tmp8[:, 2 * t + 1, :], tmp1[:, 6 + t:7 + t], gates[:, t, 0:NE],
                             ALU.mult, ALU.add))
            for i in range(4):
                eng.memset(acc[:, 2 * i:2 * i + 2, :], 0.0).then_inc(sem("acc_done"), 1)
            for i in range(4):
                bank, free = full_tile(("h2", i))
                eng.wait_ge(sem("h2_hi_done"), i + 1)
                x = (slice(None), i // 2, slice((i % 2) * 512, (i % 2 + 1) * 512))
                tt(h2_lo[x], bank[:], h2_hi[x], ALU.subtract).then_inc(free, 1)
            bank, free = full_tile("rank")
            for t in range(2):
                dve.mark(stt(keys[:, t, 0:NE], bank[:, 8 * t:8 * t + 8], 1.0, sel[:, t, :], ALU.add, ALU.mult))
            dve.sync()
            for t in range(2):
                dve.mark(ts_(keys[:, t, 0:NE], keys[:, t, 0:NE], 1.0, None, ALU.subtract))
            eng.tensor_single_scalar(tmp8[:, 0, :], bank[:, 16:24], float(P), ALU.is_gt).then_inc(free, 1)
            eng.wait_ge(free, MISC["rank"][2] + 1)
            dve.step(eng.tensor_copy(tmp8[:, 1, :], tmp8[:, 0, :]))
            a_, b_ = 1, 2
            for sh in (1, 2, 4):
                dve.mark(eng.tensor_copy(tmp8[:, b_, 0:sh], tmp8[:, a_, 0:sh]))
                dve.step(tt(tmp8[:, b_, sh:NE], tmp8[:, a_, sh:NE], tmp8[:, a_, 0:NE - sh], ALU.add))
                a_, b_ = b_, a_
            dve.mark(ts_(jobs_f[:, 0:1], tmp8[:, a_, NE - 1:NE], float(NE), None, ALU.add))
            dve.step(tt(tmp8[:, 3, :], tmp8[:, a_, :], tmp8[:, 0, :], ALU.subtract))
            dve.mark(eng.tensor_copy(jobs_f[:, 1:1 + NE], iota[:, 0:NE]))
            for r in range(JOBS - NE):
                dve.step(stt(tmp8[:, 4, :], tmp8[:, 3, :], float(r), tmp8[:, 0, :], ALU.is_equal, ALU.mult))
                for i, (x, minus, dst) in enumerate(((keys[:, 0, 0:NE], float(P), keys[:, 0, NE + r:NE + r + 1]),
                                                     (keys[:, 1, 0:NE], float(P), keys[:, 1, NE + r:NE + r + 1]),
                                                     (gates[:, 0, 0:NE], 0.0, gates[:, 0, NE + r:NE + r + 1]),
                                                     (gates[:, 1, 0:NE], 0.0, gates[:, 1, NE + r:NE + r + 1]),
                                                     (iota[:, 0:NE], 0.0, jobs_f[:, 1 + NE + r:2 + NE + r]))):
                    dve.step(stt(tmp8[:, 5, :], x, minus, tmp8[:, 4, :], ALU.subtract, ALU.mult))
                    dve.step(eng.tensor_reduce(dst, tmp8[:, 5, :], AX.X, ALU.add))
            eng.tensor_copy(jobs[:, 0:12], jobs_f[:]).then_inc(sem("jobs_ready"), 1)
            for t in range(2):
                for j in range(JOBS + 1):
                    ins = ts_(one_hot[:, t, j, :], iota[:], keys[:, t, j:j + 1], None, ALU.is_equal)
                    if (t, j) != (1, JOBS):
                        dve.mark(ins)
            ins.then_inc(sem("one_hot_ready"), 1)
            bank, free = full_tile("gslot")
            eng.tensor_copy(gslot[:, 1:1 + JOBS], bank[:, 0:JOBS]).then_inc(free, 1)

            eng.wait_ge(sem("jobs_ready"), 1)
            n_jobs = eng.value_load(jobs[0:1, 0:1], min_val=NE, max_val=JOBS)

            def gathered_lo(j):
                for half in range(2):
                    eng.wait_ge(sem("gathered"), 4 * j + half + 3)
                    eng.tensor_copy(xg_lo[:, 4 * half:4 * half + 4, :].rearrange("p k n -> p (k n)"), mi[2 + half][:])\
                        .then_inc(sem("xg_cut"), 1)

            def scaled_lo(j):
                for half in range(2):
                    eng.wait_ge(sem("ye_hi_done"), 2 * j + half + 1)
                    x = slice(half * 512, (half + 1) * 512)
                    stt(ye_lo[:, x], pj[2 + half][:], gslot[:, bass.ds(j, 1)], ye_hi[:, x], ALU.mult, ALU.subtract)\
                        .then_inc(sem("ye_lo_done"), 1)

            def add_rows(j, r):
                eng.wait_ge(sem("scattered"), 4 * j + r + 1)
                x = acc[:, 2 * r:2 * r + 2, :].rearrange("p k n -> p (k n)")
                tt(x, x, mi[2 + r % 2][:], ALU.add).then_inc(sem("acc_done"), 1)

            gathered_lo(0)
            with eng.Fori(0, n_jobs) as j:
                def cut_job_lo(n):
                    eng.wait_ge(hi_done, DENSE_UNITS + j * JU + n + 1)
                    x = (slice(None), slice(0, VM))
                    tt(mw_lo[n % HL_M][x], raw_m[n % RAW_M][x], mw_hi[n % HL_M][x], ALU.subtract).then_inc(lo_dve, 1)

                def turned_lo(st):
                    eng.wait_ge(sem("ht_hi_done"), j * STEPS + st + 1)
                    tt(ht_lo[st % 2][:].rearrange("p a n -> p (a n)"), mi[st % 2][:, 0:256],
                       ht_hi[st % 2][:].rearrange("p a n -> p (a n)"), ALU.subtract).then_inc(sem("ht_lo_done"), 1)

                for n in range(HL_M):
                    cut_job_lo(n)
                scaled_lo(j)
                for n, (kind, st) in enumerate(ORDER):
                    if kind == "B":
                        eng.wait_ge(sem("sge_done"), j * STEPS + st + 1)
                        tt(he[st % 2][:], sge[st % 2][:], pj[st % 2][:, 256:512], ALU.mult).then_inc(sem("he_done"), 1)
                    if n + HL_M < JU:
                        cut_job_lo(n + HL_M)
                    if kind == "B" and st >= 1:
                        turned_lo(st - 1)
                    if kind == "B" and st <= 1:
                        add_rows(j, 2 * st)
                        add_rows(j, 2 * st + 1)
                    if (kind, st) == ("D", STEPS - 3):
                        gathered_lo(j + 1)
                        turned_lo(STEPS - 1)
            scaled_lo(n_jobs)
            for r in range(4):
                add_rows(n_jobs, r)

            add_branch(1, 5, 8, acc, S, S, y0=S)
            for i in range(4):
                eng.wait_ge(sem("last_turned"), i + 1)
                eng.tensor_copy(fin[:, i // 2, (i % 2) * 512:(i % 2 + 1) * 512], mi[i][:]).then_inc(sem("fin_done"), 1)

        @block.gpsimd
        def _(eng):
            pool = Steps(eng, sem("pool_steps"))
            tt = eng.tensor_tensor

            def cut_pairs(first, last):
                with eng.Fori(first, last) as i:
                    for p in range(2):
                        eng.wait_ge(hi_done, 2 * i + p + 1)
                        k = slice(VK, KT)
                        tt(w_lo[p][:, k, :], raw[p][:, k, :], w_hi[p][:, k, :], ALU.subtract).then_inc(lo_pool, 1)

            def pooling(l):
                eng.wait_ge(sem("h_cut"), 8 * (2 * l + 1))
                eng.dma_start(invc[:], A["k_invc"]).then_inc(sem("invc_in"), 16)
                eng.wait_ge(pj_free[3], R_IN[l] + 3)
                eng.wait_ge(sem("invc_in"), 16 * (l + 1))
                row, pad = GRID_W + 2 * POOL_PAD, POOL_PAD
                x0_, end_ = S + 2 * pad, S + 2 * pad + ROWS * (GRID_W + 2 * pad)
                first = 0 if l == 0 else x0_
                for gi in range(4):
                    w = 2 << gi
                    a_, b_ = pads
                    grid = u[:, gi, S:T].rearrange("p (r c) -> p r c", r=ROWS)
                    dst = a_[:, x0_:end_].rearrange("p (r c) -> p r c", r=ROWS)[:, :, pad:pad + GRID_W]
                    if l or gi:
                        eng.wait_ge(sem("pooled"), 4 * l + gi)
                    pool.step(eng.memset(a_[:, first:end_], 0.0))
                    if l == 0:
                        pool.mark(eng.tensor_copy(a_[:, pad:pad + S], u[:, gi, 0:S]))
                    if w <= 4:
                        pool.step(eng.tensor_copy(dst, grid))
                        pool.step(tt(dst[:, 1:4], dst[:, 1:4], grid[:, 0:3], ALU.add))
                        if w == 4:
                            pool.step(tt(dst[:, 0:3], dst[:, 0:3], grid[:, 1:4], ALU.add))
                            pool.step(tt(dst[:, 2:4], dst[:, 2:4], grid[:, 0:2], ALU.add))
                    else:
                        pool.step(tt(b_[:, 0:2 * GRID_W], u[:, gi, S:S + 2 * GRID_W], u[:, gi, S + 2 * GRID_W:T], ALU.add))
                        both = b_[:, 0:2 * GRID_W].rearrange("p (r c) -> p r c", r=2)
                        shape = [P, ROWS, GRID_W]
                        pool.step(tt(dst, both[:, 0:1, :].to_broadcast(shape), both[:, 1:2, :].to_broadcast(shape), ALU.add))
                    sh, last = 1, end_
                    while sh < w:
                        last -= sh
                        pool.step(tt(b_[:, first:last], a_[:, first:last], a_[:, first + sh:last + sh], ALU.add))
                        a_, b_ = b_, a_
                        sh *= 2
                    at_ = pad - w // 2
                    if l == 0:
                        pool.mark(tt(b_[:, 0:S], a_[:, at_:at_ + S], invc[:, gi, 0:S], ALU.mult))
                    wide = a_[:, x0_:x0_ + ROWS * row].rearrange("p (r c) -> p r c", r=ROWS)[:, :, at_:at_ + GRID_W]
                    pool.step(tt(b_[:, S:T].rearrange("p (r c) -> p r c", r=ROWS), wide,
                                 invc[:, gi, S:T].rearrange("p (r c) -> p r c", r=ROWS), ALU.mult))
                    c0 = C0[l]
                    tt(u[:, gi, c0:T], b_[:, c0:T], u[:, gi, c0:T], ALU.subtract).then_inc(sem("pooled"), 1)
                    if gi < 3:
                        up = U_IN[l] // 2
                        cut_pairs(up + 4 + gi, up + 5 + gi)

            def halves_of(x, h):
                return x.rearrange("p e (b two h) -> p (e b) two h", two=2, h=h)

            cut_pairs(0, 1)
            for l in range(2):
                up = U_IN[l] // 2
                cut_pairs(up + 1, up + 4)
                pooling(l)
                eng.wait_ge(sem("keys_done"), 2 * l + 2)
                eng.wait_ge(sem("gate_done"), 2 * l + 2)
                for s in range(2):
                    if FULL[l, s]:
                        if (l, s) == (0, 1):
                            eng.wait_ge(mi_full, MISC[("att", 0, 0, 1, 7, 0)][1])
                        if (l, s) == (0, 0):
                            pool.mark(eng.memset(KE[0][:], 0.0))
                        tt(KE[1][:], kk[:, 0, s], kk[:, 1, s], ALU.add).then_inc(sem("diag_k"), 1)
                    for d in range(2):
                        tk = 0 if d == 0 else 1
                        for li, h in enumerate(LEVELS):
                            if not FULL[l, s]:
                                break
                            eng.wait_ge(sem("decayed"), N_EXP[l, s, d, li])
                            x = halves_of(KE[li % 2][:], h)[:, :, tk, :]
                            tt(x, x, halves_of(kk[:, d, s], h)[:, :, tk, :], ALU.mult).then_inc(sem("k_ready"), 1)
                        if s == 0:
                            eng.wait_ge(sem("decayed"), N_EXP[l, s, d, 8])
                            tt(KE[0][:], KE[0][:], kk[:, d, 0], ALU.mult).then_inc(sem("k_ready"), 1)
                cut_pairs(up + 7, (U_IN[1] // 2 + 1) if l == 0 else DENSE_UNITS // 2)
            eng.wait_ge(sem("jobs_ready"), 1)
            n_jobs = eng.value_load(jobs[0:1, 0:1], min_val=NE, max_val=JOBS)
            with eng.Fori(0, n_jobs) as j:
                for n in range(JU):
                    eng.wait_ge(hi_done, DENSE_UNITS + j * JU + n + 1)
                    x = (slice(None), slice(VM, 2048))
                    tt(mw_lo[n % HL_M][x], raw_m[n % RAW_M][x], mw_hi[n % HL_M][x], ALU.subtract).then_inc(lo_pool, 1)


def shape_constants():
    import numpy as np
    i = np.arange(P)
    masks = np.zeros((P, 14, P), np.float32)
    for li in range(7):
        h = 1 << li
        same = (i[:, None] // (2 * h)) == (i[None, :] // (2 * h))
        late = (i // h) % 2
        masks[:, li] = same & (late[:, None] == 0) & (late[None, :] == 1)
        masks[:, 7 + li] = same & (late[:, None] == 1) & (late[None, :] == 0)

    def counts(length, w):
        pos = np.arange(length)
        return np.clip(pos - w // 2 + w, 0, length) - np.clip(pos - w // 2, 0, length)

    inv = np.zeros((4, T), np.float32)
    for g in range(4):
        w = 2 << g
        inv[g, 0:S] = 1.0 / counts(S, w)
        inv[g, S:T] = (1.0 / np.outer(counts(ROWS, w), counts(GRID_W, w))).reshape(-1)
    return {
        "k_ident": np.eye(P, dtype=np.float32),
        "k_masks": masks,
        "k_ltri": (i[:, None] < i[None, :]).astype(np.float32),
        "k_iota": np.broadcast_to(i.astype(np.float32), (P, P)).copy(),
        "k_invc": np.broadcast_to(inv, (P, 4, T)).copy(),
    }


def kernel(**inputs):
    import numpy as np
    import concourse.bacc as bacc
    from concourse.bass_utils import run_bass_kernel_spmd

    arrays = {name: np.ascontiguousarray(a) for name, a in inputs.items()}
    arrays.update(shape_constants())
    nc = bacc.Bacc("TRN2", target_bir_lowering=False, num_devices=1)
    feeds, A = {}, {}
    for name, a in arrays.items():
        feeds[f"in_{name}"] = a
        A[name] = nc.dram_tensor(f"in_{name}", a.shape, mybir.dt.from_np(a.dtype), kind="ExternalInput").ap()
    A["spill"] = nc.dram_tensor("gates_spill", (16, P, T), F32, kind="Internal").ap()
    out = nc.dram_tensor("out_x", (1, S, D), F32, kind="ExternalOutput").ap()
    trunk_kernel(nc, A, out)
    r = run_bass_kernel_spmd(nc, [feeds], core_ids=[0])
    return np.asarray(r.results[0]["out_x"])
```

```python
from contextlib import ExitStack

import concourse.bass as bass
from concourse import mybir

F32 = mybir.dt.float32
F32R = mybir.dt.float32r
I32 = mybir.dt.int32
U32 = mybir.dt.uint32
U8 = mybir.dt.uint8
ALU = mybir.AluOpType
ACT = mybir.ActivationFunctionType
AX = mybir.AxisListType

P = 128
D = 1024
KT = D // P
S = 256
T = 2 * S
ROWS, GRID_W = 4, 64
HEADS = 4
HS = 128.0 ** -0.5
EPS = 1e-6
F_DENSE, F_EXP, NE = 2816, 3584, 8
FT = F_DENSE // P
LEVELS = [1 << i for i in range(8)]
POOL_PAD = 8
JOBS = 11
UC = 256
STEPS = F_EXP // 256
ORDER = []
for _st in range(STEPS):
    ORDER += [("A", _st), ("B", _st)] + ([("D", _st - 2)] if _st >= 2 else [])
ORDER += [("D", STEPS - 2), ("D", STEPS - 1)]
JU = len(ORDER)
RAW_M, HL_M = 6, 3
IN_ORDER = [1, 2, 5, 3, 4, 0, 6, 7, 8, 9]
N_IN, N_BR, N_OUT, N_GU, N_DN = 20, 4, 4, 2 * F_DENSE // UC, 12
N_ADA = 24
ADA_FIRST = 4
P_IN = [lambda i: ADA_FIRST + (2 * i + 1 if i < 6 else i + 6), None]
P_BR = [P_IN[0](N_IN // 2 - 1) + 1, None]
P_OUT = [lambda i: P_BR[0] + 2 + 2 * i + 1, None]
P_GU = lambda i: P_BR[0] + 6 + 2 * i + 1
P_DN = P_GU(N_GU // 2)
P_L1 = P_DN + N_DN // 2
P_IN[1] = lambda i: P_L1 + i
P_BR[1] = P_L1 + N_IN // 2
P_OUT[1] = lambda i: P_BR[1] + N_BR // 2 + i
DENSE_UNITS = 2 * (P_OUT[1](N_OUT // 2 - 1) + 1)


def misc_plan():
    table, used, n = {}, [0, 0, 0, 0], [0]

    def add(name, bank=None, told=1):
        b = n[0] % 4 if bank is None else bank
        table[name] = (b, n[0] + 1, used[b])
        used[b] += 1
        n[0] += told

    for k in range(KT):
        add(("xT", k))
    add("prmA")
    add("prmB")

    def ada(first, last):
        for k in range(first, last):
            add(("rows", k), 0, 0)
            add(("mod", k), 1)

    ada(0, ADA_FIRST)
    for l in range(2):
        add(("ms", l, "mix_pre"))
        if l == 0:
            ada(ADA_FIRST, ADA_FIRST + 6)
        for g in range(4):
            add(("pool", l, g))
        for s in range(2):
            full = l == 0 or s == 1
            if full:
                add(("diag", l, s, 0))
                add(("diag", l, s, 1))
            for d in range(2):
                if full:
                    for li, h in enumerate(LEVELS):
                        for tt in range(2 if h < P else 1):
                            add(("att", l, s, d, li, tt))
                if s == 0:
                    add(("kT", l, d, 0))
                    add(("kT", l, d, 1))
                    add(("st", l, d))
            if full:
                for i in range(2):
                    add(("o", l, s, i))
                for i in range(2):
                    add(("oms", l, s, i))
        if l == 0:
            ada(ADA_FIRST + 6, ADA_FIRST + 8)
        add(("ms", l, "mix_post"))
        add(("ms", l, "ffn_pre"))
        if l == 0:
            ada(ADA_FIRST + 8, N_ADA)
            add(("ms", l, "ffn_post"))
    for t in range(2):
        add(("logit", t))
    for i in range(4):
        add(("h2", i))
    add("rank")
    add("gslot")
    for j in range(JOBS):
        add(("pT", j))
    return table, n[0], used


MISC, MISC_N, MISC_USED = misc_plan()


class Steps:

    def __init__(self, eng, sem):
        self.eng, self.sem, self.k = eng, sem, 0

    def mark(self, ins):
        ins.then_inc(self.sem, 1)
        self.k += 1

    def sync(self):
        self.eng.wait_ge(self.sem, self.k)

    def step(self, ins):
        self.mark(ins)
        self.sync()


VM = 1408
VK = 6


def trunk_kernel(nc, A, out):
    with ExitStack() as ctx:
        base = (nc.sbuf_base + 63) // 64 * 64
        at = [base]

        def place(name, shape, dt, offset=None):
            size = 1 if dt == U8 else 4
            for n in shape[1:]:
                size *= n
            size = (size + 31) // 32 * 32
            if offset is None:
                offset = at[0]
                at[0] += size
            assert offset + size <= nc.sbuf_usable_end, (name, offset + size, nc.sbuf_usable_end)
            return nc.alloc_sbuf_tensor_at(name, shape, dt, offset=offset)

        K8 = 8192
        ident = place("ident", [P, P], F32)
        ones_d = place("ones_d", [P, P], F32)
        ones_h = place("ones_h", [P, P], F32)
        eps_t = place("eps_t", [P, 1], F32)
        masks = place("masks", [P, 14, P], U8)
        mod = place("mod", [P, 2, 48, 2], F32)
        prm = place("prm", [P, 96], F32)
        adab = place("adab", [P, 96], F32)
        lbp = place("lbp", [P, 6, 8], F32)
        poolw = place("poolw", [P, 4, P], F32)
        gate_st = place("gate_st", [P, T], F32, at[0] - 2048)
        csil = place("csil", [P, KT, 2], F32)
        csz = place("csz", [P, KT, 12], F32R)
        rows_sb = place("rows_sb", [8, 256], F32)
        sel_r = place("sel_r", [8, 2, 8], F32)
        craw = place("craw", [P, 2, KT], F32)
        rstd = place("rstd", [P, T], F32)
        state = place("state", [P, 2, HEADS, P], F32)
        R = place("R", [P, KT, T], F32)
        ring0 = at[0]
        raw = [place(f"raw{i}", [P, KT, UC], F32) for i in range(2)]
        w_hi = [place(f"w_hi{i}", [P, KT, UC], F32R) for i in range(2)]
        w_lo = [place(f"w_lo{i}", [P, KT, UC], F32R) for i in range(2)]
        h0 = at[0]
        h_hi = place("h_hi", [P, KT, T], F32R)
        h_lo = place("h_lo", [P, KT, T], F32R)
        z0 = at[0]
        q = place("q", [P, 2, HEADS, S], F32)
        lf = place("lf", [P, 2, 2, HEADS, S], F32)
        kk = place("kk", [P, 2, 2, HEADS, S], F32)
        v = place("v", [P, 4, 512], F32)
        g = place("g", [P, HEADS, T], F32)
        u = place("u", [P, HEADS, T], F32)
        x0 = at[0]
        cA = place("cA", [P, HEADS, S], F32)
        cB = place("cB", [P, HEADS, S], F32)
        QE = [place(f"QE{i}", [P, HEADS, S], F32) for i in range(2)]
        KE = [place(f"KE{i}", [P, HEADS, S], F32) for i in range(2)]
        att = place("att", [P, 2, HEADS, S], F32)
        end = at[0]
        gE = place("gE", [P, 2, HEADS, S], F32, x0 + 8192)
        gL = place("gL", [P, 2, HEADS, S], F32, x0 + 16384)
        invc = place("invc", [P, 4, T], F32, x0 + 24576)
        pads = [place(f"pad{i}", [P, 1024], F32, x0 + 4096 * i) for i in range(2)]
        yr_hi = place("yr_hi", [P, 4, T], F32R, h0)
        yr_lo = place("yr_lo", [P, 4, T], F32R, h0 + K8)
        yp_hi = place("yp_hi", [P, 4, T], F32R, h0 + 2 * K8)
        yp_lo = place("yp_lo", [P, 4, T], F32R, h0 + 3 * K8)
        m_hi = place("m_hi", [P, KT, T], F32R, z0)
        m_lo = place("m_lo", [P, KT, T], F32R, z0 + 2 * K8)
        sgate = [place(f"sgate{i}", [P, 2, 2, T], F32, z0 + 4 * K8 + K8 * i) for i in range(2)]
        mt = [place(f"mt{i}", [P, T], F32, z0 + 6 * K8 + 2048 * i) for i in range(4)]
        Y = place("Y", [P, KT, T], F32, z0 + 8 * K8)
        SQ = place("SQ", [P, KT, T], F32, z0 + 10 * K8)
        HF = SQ
        hid_hi = place("hid_hi", [P, FT, T], F32R, z0)
        hid_lo = place("hid_lo", [P, FT, T], F32R, z0 + 2048 * FT)
        sg = place("sg", [P, 2, T], F32, z0 + 4096 * FT)
        hf = place("hf", [P, 2, T], F32, z0 + 4096 * FT + 4096)
        Y2 = place("Y2", [P, KT, T], F32, h0)
        SQ2 = place("SQ2", [P, KT, T], F32, h0 + 2 * K8)
        xin = place("xin", [P, 4, D], F32, h0)
        rowsA = place("rowsA", [96, P], F32, h0 + 2 * K8)
        rowsB = place("rowsB", [96, P], F32, h0 + 2 * K8 + 512)
        masks_f = place("masks_f", [P, 14, P], F32, z0 + 4 * K8)
        raw_m = [place(f"raw_m{i}", [P, 2048], F32, ring0 + K8 * i) for i in range(RAW_M)]
        m0 = h0
        mw_hi = [place(f"mw_hi{i}", [P, 2048], F32R, m0 + K8 * 2 * i) for i in range(HL_M)]
        mw_lo = [place(f"mw_lo{i}", [P, 2048], F32R, m0 + K8 * (2 * i + 1)) for i in range(HL_M)]
        mo = [m0 + 2 * K8 * HL_M]

        def moe(name, shape, dt):
            size = 4
            for n in shape[1:]:
                size *= n
            t = place(name, shape, dt, mo[0])
            mo[0] += size
            assert mo[0] <= end
            return t

        one_hot = moe("one_hot", [P, 2, JOBS + 1, P], F32R)
        scat = moe("scat", [P, JOBS + 1, S], F32R)
        acc = moe("acc", [P, KT, S], F32)
        h2_hi = moe("h2_hi", [P, 2, D], F32R)
        h2_lo = moe("h2_lo", [P, 2, D], F32R)
        xg_hi = moe("xg_hi", [P, KT, P], F32R)
        xg_lo = moe("xg_lo", [P, KT, P], F32R)
        he = [moe(f"he{i}", [P, 256], F32) for i in range(2)]
        sge = [moe(f"sge{i}", [P, 256], F32) for i in range(2)]
        ht_hi = [moe(f"ht_hi{i}", [P, 2, P], F32R) for i in range(2)]
        ht_lo = [moe(f"ht_lo{i}", [P, 2, P], F32R) for i in range(2)]
        ye_hi = moe("ye_hi", [P, D], F32R)
        ye_lo = moe("ye_lo", [P, D], F32R)
        HM = place("HM", [P, KT, S], F32, m0)
        rt0 = m0 + K8
        rw = place("rw", [P, KT, NE], F32, rt0)
        ltri = place("ltri", [P, P], F32, rt0 + 512)
        iota = place("iota", [P, P], F32, rt0 + 1024)
        ones_1 = place("ones_1", [P, P], F32, rt0 + 1536)
        lg = place("lg", [P, 2, NE], F32, rt0 + 2048)
        top_v = place("top_v", [P, 2, 8], F32, rt0 + 2112)
        top_i = place("top_i", [P, 2, 8], U32, rt0 + 2176)
        top_f = place("top_f", [P, 2, 8], F32, rt0 + 2240)
        sel = place("sel", [P, 2, NE], F32, rt0 + 2304)
        gates = place("gates", [P, 2, 12], F32, rt0 + 2368)
        keys = place("keys", [P, 2, 12], F32, rt0 + 2464)
        tmp8 = place("tmp8", [P, 8, NE], F32, rt0 + 2560)
        tmp1 = place("tmp1", [P, 32], F32, rt0 + 2816)
        gslot = place("gslot", [P, 12], F32, None)
        jobs_f = place("jobs_f", [P, 12], F32, rt0 + 3072)
        jobs = place("jobs", [P, 16], I32, None)
        fin = place("fin", [P, 2, D], F32, h0)
        SQM = place("SQM", [P, KT, S], F32, m0 + 2 * K8 * HL_M + 32768)

        pj = [ctx.enter_context(nc.psum_tensor(f"pj{i}", [P, 512], F32)) for i in range(4)]
        mi = [ctx.enter_context(nc.psum_tensor(f"mi{i}", [P, 512], F32)) for i in range(4)]

        names = {}

        def sem(name):
            if name not in names:
                names[name] = ctx.enter_context(nc.semaphore(name))
            return names[name]

        unit_used = sem("unit_used")
        hi_done, lo_dve, lo_pool = sem("hi_done"), sem("lo_dve"), sem("lo_pool")
        raw_in = [sem(f"raw_in{i}") for i in range(2)]
        rawm_in = [sem(f"rawm_in{i}") for i in range(RAW_M)]
        pj_free = [sem(f"pj_free{i}") for i in range(4)]
        mi_free = [sem(f"mi_free{i}") for i in range(4)]
        mi_full = sem("mi_full")

        def mi_of(name):
            b, full, before = MISC[name]
            return mi[b], mi_free[b], full, before

        def ADA_USED(k, i):
            if k < ADA_FIRST:
                pair = k
            elif k < ADA_FIRST + 6:
                pair = P_IN[0](k - ADA_FIRST) - 1
            elif k < ADA_FIRST + 8:
                pair = P_OUT[0](k - ADA_FIRST - 6) - 1
            else:
                pair = P_DN - 1 if k == N_ADA - 1 else P_GU(i) - 1
            return 2 * pair + 2

        def kept_keys(d):
            return kk[:, d, 0].rearrange("p e t -> p (e t)").rearrange("p (t e n) -> p t e n", t=2, e=HEADS)

        C0 = [0, S]
        NT = [T, S]
        L0_ROUNDS = 10 + 4 + 2 + 11 + 2
        R_IN, R_BR, R_OUT = ([b + x for b in (0, L0_ROUNDS)] for x in (0, 10, 14))
        R_GU, R_DN = 16, 27
        SCANS = [(l, s, d) for l in range(2) for s in range(2) for d in range(2)]
        FULL = {(l, s): l == 0 or s == 1 for l in range(2) for s in range(2)}

        def number(keep):
            keys = [k + (li,) for k in SCANS for li in range(9) if keep(*k, li)]
            return {k: n + 1 for n, k in enumerate(keys)}

        N_EXP = number(lambda l, s, d, li: FULL[l, s] or li == 8)
        N_Q = number(lambda l, s, d, li: FULL[l, s] and (li < 8 or s == 1))
        N_K = number(lambda l, s, d, li: (FULL[l, s] and li < 8) or (s == 0 and li == 8))

        spill = A["spill"]
        w_in_src = A["w_in"].rearrange("l (k p) n -> l p k n", p=P)
        rec_src = A["w_branch_rec"].rearrange("l (k p) n -> l p k n", p=P)
        pool_src = A["w_branch_pool"].rearrange("l (k p) n -> l p k n", p=P)
        out_src = A["w_out"].rearrange("l (k p) n -> l p k n", p=P)
        gate_src = A["ffn_w_gate"].rearrange("l (k p) n -> l p k n", p=P)[0]
        up_src = A["ffn_w_up"].rearrange("l (k p) n -> l p k n", p=P)[0]
        down_src = A["ffn_w_down"].rearrange("l (k p) n -> l p k n", p=P)[0]
        ada_src = A["ada_w"].rearrange("l (p k) n -> l p k n", k=KT)
        eg_src = A["moe_w_gate"][0]
        eu_src = A["moe_w_up"][0]
        ed_src = A["moe_w_down"][0]

        block = ctx.enter_context(nc.Block())

        @block.sync
        def _(eng):
            for t in range(4):
                src = (A["ctx"], A["x"])[t // 2][0, (t % 2) * P:(t % 2 + 1) * P, :]
                eng.dma_start(xin[:, t, :], src).then_inc(sem("x_in"), 16)
            eng.dma_start(ident[:], A["k_ident"]).then_inc(sem("consts_in"), 16)
            eng.dma_start(masks_f[:], A["k_masks"]).then_inc(sem("consts_in"), 16)
            eng.dma_start(sel_r[:], A["k_sel"].rearrange("p (a n) -> p a n", a=2)).then_inc(sem("consts_in"), 16)
            eng.dma_start(rowsA[:], A["ada_b"].rearrange("l (c p) -> (l c) p", p=P)).then_inc(sem("rows_in"), 16)
            row = 0
            for name in ("mix_pre", "mix_post", "ffn_pre", "ffn_post", "hgrn_lb", "hgrn_gain", "pool_scale"):
                src = A[name]
                if name == "hgrn_lb":
                    src = src.rearrange("l d (c p) -> (l d c) p", p=P)
                else:
                    src = src.rearrange("l (c p) -> (l c) p", p=P)
                eng.dma_start(rowsB[row:row + src.shape[0], :], src).then_inc(sem("rows_in"), 16)
                row += src.shape[0]
            eng.dma_start(craw[:, 0, :], A["c_ctx"].rearrange("(p k) -> p k", k=KT)).then_inc(sem("c_in"), 16)
            eng.dma_start(craw[:, 1, :], A["c"].rearrange("b (p k) -> p (b k)", k=KT)).then_inc(sem("c_in"), 16)

            def load(pair, p, parts):
                if not isinstance(pair, int) or pair > 0:
                    eng.wait_ge(lo_dve, 2 * pair + p - 1)
                    eng.wait_ge(lo_pool, 2 * pair + p - 1)
                k = 0
                for n, (src, kts) in enumerate(parts):
                    eng.dma_start(raw[p][:, k:k + kts, :], src)\
                       .then_inc(raw_in[p], 16 if n < len(parts) - 1 else 16 * (3 - len(parts)))
                    k += kts

            def load_gates(l, b):
                if b == 0:
                    eng.wait_ge(sem("spilled"), 16 * 16 * (l + 1))
                    eng.wait_ge(sem("branches_cut"), 4 * (l + 1))
                if b >= 2:
                    eng.wait_ge(pj_free[3], R_BR[l] + b - 1)
                for i in range(2):
                    eng.dma_start(sgate[b % 2][:, i, :, 0:NT[l]],
                                  spill[8 * i + 2 * b:8 * i + 2 * b + 2, :, 0:NT[l]].rearrange("t p n -> p t n"))\
                       .then_inc(sem(f"gates_in{b % 2}"), 16)

            def load_ada(pair, k):
                l = (k if isinstance(k, int) else 12) // 12
                for p in range(2):
                    load(pair, p, [(ada_src[l][:, :, bass.ds((k - 12 * l) * 2 * UC + p * UC, UC)], KT)])

            for k in range(ADA_FIRST):
                load_ada(k, k)
            for l in range(2):
                if l == 0:
                    eng.dma_start(poolw[:], A["pool_w"][0].rearrange("g c e -> c g e")).then_inc(sem("poolw_in"), 16)
                for i in range(6):
                    if l == 0:
                        load_ada(P_IN[0](i) - 1, ADA_FIRST + i)
                    for p in range(2):
                        c = IN_ORDER[i] * 2 * UC + p * UC
                        load(P_IN[l](i), p, [(w_in_src[l][:, :, c:c + UC], KT)])
                with eng.Fori(0, 4) as i:
                    for p in range(2):
                        load(P_IN[l](6) + i, p, [(w_in_src[l][:, :, bass.ds((2 * i + 12 + p) * UC, UC)], KT)])
                for b in range(N_BR):
                    cols = slice(b * UC, (b + 1) * UC)
                    load(P_BR[l] + b // 2, b % 2, [(rec_src[l][:, :, cols], 4), (pool_src[l][:, :, cols], 4)])
                    if b >= 1:
                        load_gates(l, b - 1)
                load_gates(l, 3)
                if l == 0:
                    eng.wait_ge(mi_full, MISC[("pool", 0, 3)][1])
                    eng.dma_start(poolw[:], A["pool_w"][1].rearrange("g c e -> c g e")).then_inc(sem("poolw_in"), 16)
                for n in range(N_OUT):
                    if l == 0 and n % 2 == 0:
                        load_ada(P_OUT[0](n // 2) - 1, ADA_FIRST + 6 + n // 2)
                    load(P_OUT[l](n // 2), n % 2, [(out_src[l][:, :, n * UC:(n + 1) * UC], KT)])
                if l == 0:
                    with eng.Fori(0, N_GU // 2) as i:
                        load_ada(P_GU(i) - 1, ADA_FIRST + 8 + i)
                        load(P_GU(i), 0, [(gate_src[:, :, bass.ds(i * UC, UC)], KT)])
                        load(P_GU(i), 1, [(up_src[:, :, bass.ds(i * UC, UC)], KT)])
                    load_ada(P_DN - 1, N_ADA - 1)
                    with eng.Fori(0, 2) as i:
                        for n in range(6):
                            k0, kts = 8 * (n % 3), (8, 8, 6)[n % 3]
                            load(P_DN + 3 * i + n // 2, n % 2,
                                 [(down_src[:, k0:k0 + kts, bass.ds((2 * i + n // 3) * UC, UC)], kts)])

            eng.wait_ge(unit_used, DENSE_UNITS)
            eng.dma_start(rw[:], A["moe_router"][0].rearrange("(k p) e -> p k e", p=P)).then_inc(sem("route_in"), 16)
            eng.dma_start(ltri[:], A["k_ltri"]).then_inc(sem("route_in"), 16)
            eng.dma_start(iota[:], A["k_iota"]).then_inc(sem("route_in"), 16)
            eng.wait_ge(sem("jobs_ready"), 1)
            n_jobs = eng.value_load(jobs[0:1, 0:1], min_val=NE, max_val=JOBS)
            with eng.Fori(0, n_jobs) as j:
                expert = eng.value_load(jobs[0:1, bass.ds(j + 1, 1)], min_val=0, max_val=NE - 1)
                for n, (kind, st) in enumerate(ORDER):
                    slot = raw_m[n % RAW_M]
                    eng.wait_ge(lo_dve, DENSE_UNITS + j * JU + n - RAW_M + 1)
                    eng.wait_ge(lo_pool, DENSE_UNITS + j * JU + n - RAW_M + 1)
                    if kind == "D":
                        src = ed_src[bass.ds(expert, 1), st * 256:(st + 1) * 256, :]\
                            .rearrange("e (k p) n -> p (e k) n", p=P)
                        eng.dma_start(slot[:].rearrange("p (k n) -> p k n", k=2), src)\
                           .then_inc(rawm_in[n % RAW_M], 32)
                    else:
                        k0 = 0 if kind == "A" else 512
                        dst = slot[:].rearrange("p (k h n) -> p k h n", k=4, h=2)
                        for half, w in enumerate((eg_src, eu_src)):
                            src = w[bass.ds(expert, 1), k0:k0 + 512, st * 256:(st + 1) * 256]\
                                .rearrange("e (k p) n -> p (e k) n", p=P)
                            eng.dma_start(dst[:, :, half, :], src).then_inc(rawm_in[n % RAW_M], 16)
            eng.wait_ge(sem("fin_done"), 4)
            for t in range(2):
                eng.dma_start(out[0, t * P:(t + 1) * P, :], fin[:, t, :]).then_inc(sem("stored"), 16)
            eng.wait_ge(sem("stored"), 32)

        @block.tensor
        def _(eng):
            told = [0]

            def tile(name):
                bank, free, full, before = mi_of(name)
                assert full == told[0] + 1, name
                if before:
                    eng.wait_ge(free, before)
                return bank

            def filled(ins):
                ins.then_inc(mi_full, 1)
                told[0] += 1

            eng.wait_ge(sem("x_in"), 64)
            eng.wait_ge(sem("consts_in"), 48)
            for k in range(KT):
                bank = tile(("xT", k))
                for t in range(4):
                    ins = eng.transpose(bank[:, t * P:(t + 1) * P], xin[:, t, k * P:(k + 1) * P], ident[:])
                filled(ins)
            eng.wait_ge(sem("rows_in"), 16 * 8)
            filled(eng.transpose(tile("prmA")[:, 0:96], rowsA[:], ident[0:96, 0:96]))
            filled(eng.transpose(tile("prmB")[:, 0:96], rowsB[:], ident[0:96, 0:96]))
            def passes(dst, ah, al, bh, bl, first, last):
                eng.matmul(dst, ah, bh, start=first, stop=False)
                eng.matmul(dst, ah, bl, start=False, stop=False)
                return eng.matmul(dst, al, bh, start=False, stop=last)

            def unit_in(pair, p):
                eng.wait_ge(lo_dve, 2 * pair + p + 1)
                eng.wait_ge(lo_pool, 2 * pair + p + 1)

            def bank_free(b, rounds):
                if not isinstance(rounds, int) or rounds > 0:
                    eng.wait_ge(pj_free[b], rounds)

            def ada(pair, k, i=0):
                b, full, before = MISC[("rows", k)]
                eng.wait_ge(mi_free[b], before + i)
                for p in range(2):
                    unit_in(pair, p)
                    for kt in range(KT):
                        for w in (w_hi, w_lo):
                            ins = eng.matmul(mi[b][0:8, 0:UC], csz[:, kt, 4 - 4 * p:12 - 4 * p], w[p][:, kt, :],
                                             start=(p == 0 and kt == 0 and w is w_hi),
                                             stop=(p == 1 and kt == KT - 1 and w is w_lo))
                    if p == 0:
                        ins.then_inc(unit_used, 1)
                ins.then_inc(unit_used, 1)

            def ada_turn(k, i=0):
                b, full, before = MISC[("mod", k)]
                eng.wait_ge(mi_free[b], before + i)
                b0, _, before0 = MISC[("rows", k)]
                eng.wait_ge(mi_free[b0], before0 + i + 1)
                for h in range(2):
                    ins = eng.matmul(mi[b][:, 0:8], rows_sb[:, h * P:(h + 1) * P], sel_r[:, h, :],
                                     start=(h == 0), stop=(h == 1))
                filled(ins)

            def half_unit(pair, rounds, c0, n, e, xh=h_hi, xl=h_lo, cut=None):
                p, j = e // 2, e % 2
                if j == 0:
                    unit_in(pair, p)
                bank_free(e, rounds)
                for k in range(KT):
                    if cut and e == 0:
                        eng.wait_ge(cut[0], cut[1] + k + 1)
                    w = slice(j * P, (j + 1) * P)
                    ins = passes(pj[e][:, 0:n], w_hi[p][:, k, w], w_lo[p][:, k, w],
                                 xh[:, k, c0:c0 + n], xl[:, k, c0:c0 + n], k == 0, k == KT - 1)
                if j == 1:
                    ins.then_inc(unit_used, 1)

            def project(pair, rounds, c0, n, xh=h_hi, xl=h_lo, between=None, cut=None):
                for e in range(4):
                    half_unit(pair, rounds, c0, n, e, xh, xl, cut)
                    if e == 1 and between:
                        between()

            def project_tokens(pair, rounds, between=None):
                for p in range(2):
                    unit_in(pair, p)
                    for t in range(4):
                        if p == 0:
                            bank_free(t, rounds)
                        for k in range(KT):
                            x = slice(t * P, (t + 1) * P)
                            ins = passes(pj[t][:, p * UC:(p + 1) * UC], h_hi[:, k, x], h_lo[:, k, x],
                                         w_hi[p][:, k, :], w_lo[p][:, k, :], k == 0, k == KT - 1)
                    ins.then_inc(unit_used, 1)
                    if p == 0 and between:
                        between()

            def mean_square(name, sq, c0, n, seen):
                bank = tile(name)
                for k in range(KT):
                    eng.wait_ge(sem("squared"), seen + k + 1)
                    ins = eng.matmul(bank[:, 0:n], ones_d[:], sq[:, k, c0:c0 + n], start=(k == 0), stop=(k == KT - 1))
                filled(ins)

            def scan_products(l, s, d):
                pair = 2 * s + d
                gates_of = (P_IN[l](6 + pair), R_IN[l] + 6 + pair, C0[l], NT[l])
                if not FULL[l, s]:
                    project(*gates_of)
                if FULL[l, s]:
                    for li, h in enumerate(LEVELS):
                        eng.wait_ge(sem("q_ready"), N_Q[l, s, d, li])
                        eng.wait_ge(sem("k_ready"), N_K[l, s, d, li])
                        qe, ke = QE[li % 2], KE[li % 2]
                        for tt in range(2 if h < P else 1):
                            bank = tile(("att", l, s, d, li, tt))
                            st, qt = (tt, tt) if h < P else ((0, 1) if d == 0 else (1, 0))
                            for hd in range(HEADS):
                                ins = eng.matmul(bank[:, hd * P:(hd + 1) * P], ke[:, hd, st * P:(st + 1) * P],
                                                 qe[:, hd, qt * P:(qt + 1) * P], start=True, stop=True)
                            filled(ins)
                        if li % 2:
                            half_unit(*gates_of, li // 2)
                if s == 0:
                    eng.wait_ge(sem("k_ready"), N_K[l, s, d, 8])
                    for t in range(2):
                        bank = tile(("kT", l, d, t))
                        for hd in range(HEADS):
                            ins = eng.transpose(bank[:, hd * P:(hd + 1) * P], KE[0][:, hd, t * P:(t + 1) * P], ident[:])
                        filled(ins)
                    b1, _, kept1 = MISC[("kT", l, d, 1)]
                    eng.wait_ge(mi_free[b1], kept1 + 1)
                    bank = tile(("st", l, d))
                    for hd in range(HEADS):
                        for t in range(2):
                            ins = eng.matmul(bank[:, hd * P:(hd + 1) * P], kept_keys(d)[:, t, hd, :],
                                             v[:, t, hd * P:(hd + 1) * P], start=(t == 0), stop=(t == 1))
                    filled(ins)

            def token_mix(l):
                c0, n = C0[l], NT[l]
                eng.wait_ge(sem("poolw_in"), 16 * (l + 1))
                eng.wait_ge(sem("pooled"), 4 * (l + 1))
                for gi in range(4):
                    filled(eng.matmul(tile(("pool", l, gi))[:, 0:n], poolw[:, gi, :], u[:, gi, c0:c0 + n],
                                      start=True, stop=True))
                for s in range(2):
                    if FULL[l, s]:
                        eng.wait_ge(sem("diag_q"), l + s + 1 if l == 0 else 3)
                        eng.wait_ge(sem("diag_k"), l + s + 1 if l == 0 else 3)
                        for t in range(2):
                            bank = tile(("diag", l, s, t))
                            for hd in range(HEADS):
                                ins = eng.matmul(bank[:, hd * P:(hd + 1) * P], KE[1][:, hd, t * P:(t + 1) * P],
                                                 QE[1][:, hd, t * P:(t + 1) * P], start=True, stop=True)
                            filled(ins)
                    for d in range(2):
                        scan_products(l, s, d)
                    if not FULL[l, s]:
                        continue
                    ba, _, before = MISC[("att", l, s, 1, 7, 0)]
                    eng.wait_ge(mi_free[ba], before + 1)
                    if s == 1:
                        bs, _, before = MISC[("st", l, 1)]
                        eng.wait_ge(mi_free[bs], before + 1)
                        eng.wait_ge(sem("q_ready"), N_Q[l, s, 1, 8])
                    for i in range(2):
                        bank = tile(("o", l, s, i))
                        for hd in (2 * i, 2 * i + 1):
                            dst = bank[:, (hd % 2) * S:(hd % 2 + 1) * S]
                            for t in range(2):
                                ins = eng.matmul(dst, v[:, 2 * s + t, hd * P:(hd + 1) * P], att[:, t, hd, :],
                                                 start=(t == 0), stop=(t == 1 and s == 0))
                            if s == 1:
                                for d in range(2):
                                    ins = eng.matmul(dst, state[:, d, hd, :], lf[:, d, 1, hd, :],
                                                     start=False, stop=(d == 1))
                        filled(ins)
                    for i in range(2):
                        eng.wait_ge(sem("o_squared"), 2 * (l + s if l == 0 else 2) + i + 1)
                        bank = tile(("oms", l, s, i))
                        filled(eng.matmul(bank[:], ones_h[:], cA[:, 2 * i:2 * i + 2, :].rearrange("p h t -> p (h t)"),
                                          start=True, stop=True))

            SQ_SEEN = {(0, "mix_pre"): 0, (0, "mix_post"): 8, (0, "ffn_pre"): 16, (0, "ffn_post"): 24,
                       (1, "mix_pre"): 32, (1, "mix_post"): 40, (1, "ffn_pre"): 48}
            eng.wait_ge(sem("ones_set"), 3)
            eng.wait_ge(sem("csz_set"), 2)
            for k in range(ADA_FIRST):
                ada(k, k)
                ada_turn(k)
            for l in range(2):
                c0, n = C0[l], NT[l]
                mean_square(("ms", l, "mix_pre"), SQ, 0, T, SQ_SEEN[l, "mix_pre"])
                ur = R_IN[l]
                for i in range(6):
                    turn_k = None
                    if l == 0:
                        ada(P_IN[0](i) - 1, ADA_FIRST + i)
                        turn_k = lambda k=ADA_FIRST + i: ada_turn(k)
                    if i == 3:
                        project_tokens(P_IN[l](3), ur + 3, turn_k)
                    else:
                        project(P_IN[l](i), ur + i, *((0, T) if i < 2 else (c0, n)), between=turn_k,
                                cut=None if i else (sem("h_cut"), 16 * l))
                token_mix(l)
                eng.wait_ge(sem("branches_cut"), 4 * (l + 1))
                for b in range(N_BR):
                    unit_in(P_BR[l] + b // 2, b % 2)
                    for br, (yh, yl) in enumerate(((yr_hi, yr_lo), (yp_hi, yp_lo))):
                        for j in range(2):
                            bank_free(2 * br + j, R_BR[l] + b)
                            for k in range(4):
                                w = (slice(None), 4 * br + k, slice(j * P, (j + 1) * P))
                                ins = passes(pj[2 * br + j][:, 0:n], w_hi[b % 2][w], w_lo[b % 2][w],
                                             yh[:, k, c0:c0 + n], yl[:, k, c0:c0 + n], k == 0, k == 3)
                    ins.then_inc(unit_used, 1)
                for i in range(2):
                    turn_k = None
                    if l == 0:
                        ada(P_OUT[0](i) - 1, ADA_FIRST + 6 + i)
                        turn_k = lambda k=ADA_FIRST + 6 + i: ada_turn(k)
                    project(P_OUT[l](i), R_OUT[l] + i, c0, n, m_hi, m_lo, turn_k, None if i else (sem("m_cut"), 8 * l))
                mean_square(("ms", l, "mix_post"), SQ, c0, n, SQ_SEEN[l, "mix_post"])
                mean_square(("ms", l, "ffn_pre"), SQ, c0, n, SQ_SEEN[l, "ffn_pre"])
                if l == 0:
                    with eng.Fori(0, N_GU // 2) as i:
                        ada(P_GU(i) - 1, ADA_FIRST + 8, i)
                        project(P_GU(i), R_GU + i, 0, T, between=lambda: ada_turn(ADA_FIRST + 8, i), cut=(sem("h_cut"), 8))
                    ada(P_DN - 1, N_ADA - 1)
                    ada_turn(N_ADA - 1)
                    told[0] = MISC[("mod", N_ADA - 1)][1]
                    eng.wait_ge(sem("hid_cut"), FT)
                    with eng.Fori(0, 2) as i:
                        for n6 in range(6):
                            gr, pc = n6 // 3, n6 % 3
                            unit_in(P_DN + 3 * i + n6 // 2, n6 % 2)
                            for j in range(2):
                                if pc == 0:
                                    bank_free(2 * gr + j, R_DN + i)
                                kts = (8, 8, 6)[pc]
                                for k in range(kts):
                                    w = (slice(None), k, slice(j * P, (j + 1) * P))
                                    ins = passes(pj[2 * gr + j][:], w_hi[n6 % 2][w], w_lo[n6 % 2][w],
                                                 hid_hi[:, 8 * pc + k, :], hid_lo[:, 8 * pc + k, :],
                                                 pc == 0 and k == 0, pc == 2 and k == kts - 1)
                            ins.then_inc(unit_used, 1)
                    mean_square(("ms", l, "ffn_post"), SQ2, 0, T, SQ_SEEN[l, "ffn_post"])

            eng.wait_ge(sem("route_in"), 48)
            eng.wait_ge(sem("hm_ready"), KT)
            for t in range(2):
                bank = tile(("logit", t))
                for k in range(KT):
                    ins = eng.matmul(bank[:, 0:NE], HM[:, k, t * P:(t + 1) * P], rw[:, k, :],
                                     start=(k == 0), stop=(k == KT - 1))
                filled(ins)
            for i in range(4):
                bank = tile(("h2", i))
                for k in range(4):
                    kt = 4 * (i % 2) + k
                    ins = eng.transpose(bank[:, k * P:(k + 1) * P], HM[:, kt, (i // 2) * P:(i // 2 + 1) * P], ident[:])
                filled(ins)
            eng.wait_ge(sem("sel_ready"), 1)
            bank = tile("rank")
            eng.matmul(bank[:, 0:8], ltri[:], sel[:, 0, :], start=True, stop=True)
            eng.matmul(bank[:, 8:16], ltri[:], sel[:, 1, :], start=True, stop=False)
            eng.matmul(bank[:, 8:16], ones_1[:], sel[:, 0, :], start=False, stop=True)
            eng.matmul(bank[:, 16:24], ones_1[:], sel[:, 0, :], start=True, stop=False)
            filled(eng.matmul(bank[:, 16:24], ones_1[:], sel[:, 1, :], start=False, stop=True))
            eng.wait_ge(sem("one_hot_ready"), 1)
            bank = tile("gslot")
            for j in range(JOBS):
                for t in range(2):
                    ins = eng.matmul(bank[:, j:j + 1], one_hot[:, t, j, :].bitcast(F32), gates[:, t, j:j + 1],
                                     start=(t == 0), stop=(t == 1))
            filled(ins)
            for j in range(JOBS):
                bank = tile(("pT", j))
                for t in range(2):
                    ins = eng.transpose(bank[:, t * P:(t + 1) * P], one_hot[:, t, j, :].bitcast(F32), ident[:])
                filled(ins)
            assert told[0] == MISC_N

            eng.wait_ge(sem("jobs_ready"), 1)
            for b in range(4):
                eng.wait_ge(mi_free[b], MISC_USED[b])
            n_jobs = eng.value_load(jobs[0:1, 0:1], min_val=NE, max_val=JOBS)
            def gather(j, h2, half):
                bank = mi[2 + half]
                for k in range(4):
                    kt = 4 * half + k
                    for t in range(2):
                        ins = eng.matmul(bank[:, k * P:(k + 1) * P], h2[:, t, kt * P:(kt + 1) * P],
                                         one_hot[:, t, bass.ds(j, 1), :].rearrange("p a n -> p (a n)"),
                                         start=(t == 0), stop=(t == 1))
                ins.then_inc(sem("gathered"), 1)

            def scatter(j, r):
                if r >= 2:
                    eng.wait_ge(sem("acc_done"), 4 * j + r + 3)
                for k in range(2):
                    kt = 2 * r + k
                    dst = mi[2 + r % 2][:, k * S:(k + 1) * S]
                    sc = scat[:, bass.ds(j, 1), :].rearrange("p a n -> p (a n)")
                    eng.matmul(dst, ye_hi[:, kt * P:(kt + 1) * P], sc, start=True, stop=False)
                    ins = eng.matmul(dst, ye_lo[:, kt * P:(kt + 1) * P], sc, start=False, stop=True)
                ins.then_inc(sem("scattered"), 1)

            with eng.Fori(0, 1) as j:
                for half in range(2):
                    gather(j, h2_hi, half)
                for half in range(2):
                    eng.wait_ge(sem("xg_hi_done"), half + 1)
                    gather(j, h2_lo, half)
            with eng.Fori(0, n_jobs) as j:
                def down(n, st):
                    eng.wait_ge(lo_dve, DENSE_UNITS + j * JU + n + 1)
                    eng.wait_ge(lo_pool, DENSE_UNITS + j * JU + n + 1)
                    eng.wait_ge(sem("ht_lo_done"), j * STEPS + st + 1)
                    for half in range(2):
                        for t2 in range(2):
                            w = slice(t2 * D + half * 512, t2 * D + half * 512 + 512)
                            ins = passes(pj[2 + half][:], ht_hi[st % 2][:, t2, :], ht_lo[st % 2][:, t2, :],
                                         mw_hi[n % HL_M][:, w], mw_lo[n % HL_M][:, w],
                                         st == 0 and t2 == 0, st == STEPS - 1 and t2 == 1)
                    ins.then_inc(unit_used, 1)

                def turn(st):
                    eng.wait_ge(sem("he_done"), j * STEPS + st + 1)
                    if st >= 2:
                        eng.wait_ge(sem("ht_lo_done"), j * STEPS + st - 1)
                    for t2 in range(2):
                        ins = eng.transpose(mi[st % 2][:, t2 * P:(t2 + 1) * P], he[st % 2][:, t2 * P:(t2 + 1) * P],
                                            ident[:])
                    ins.then_inc(sem("turned"), 1)

                eng.wait_ge(sem("xg_cut"), 2 * j + 2)
                for n, (kind, st) in enumerate(ORDER):
                    if kind == "D":
                        if st == STEPS - 2:
                            for half in range(2):
                                eng.wait_ge(sem("xg_hi_done"), 2 * j + 3 + half)
                                gather(j + 1, h2_lo, half)
                            turn(STEPS - 1)
                        down(n, st)
                        continue
                    eng.wait_ge(lo_dve, DENSE_UNITS + j * JU + n + 1)
                    eng.wait_ge(lo_pool, DENSE_UNITS + j * JU + n + 1)
                    if kind == "A" and st >= 2:
                        eng.wait_ge(sem("he_done"), j * STEPS + st - 1)
                    for k in range(4):
                        kt = k + (0 if kind == "A" else 4)
                        ins = passes(pj[st % 2][:], xg_hi[:, kt, :], xg_lo[:, kt, :],
                                     mw_hi[n % HL_M][:, k * 512:(k + 1) * 512],
                                     mw_lo[n % HL_M][:, k * 512:(k + 1) * 512],
                                     kt == 0, kt == KT - 1)
                    ins.then_inc(unit_used, 1)
                    if kind == "B" and st >= 1:
                        turn(st - 1)
                    if kind == "B" and st <= 1:
                        if st == 0:
                            eng.wait_ge(sem("ye_lo_done"), 2 * j + 2)
                        scatter(j, 2 * st)
                        scatter(j, 2 * st + 1)
                    if (kind, st) == ("B", STEPS - 1):
                        eng.wait_ge(sem("acc_done"), 4 * j + 8)
                        for half in range(2):
                            gather(j + 1, h2_hi, half)
            eng.wait_ge(sem("ye_lo_done"), n_jobs * 2 + 2)
            eng.wait_ge(sem("xg_cut"), n_jobs * 2 + 2)
            for r in range(4):
                scatter(n_jobs, r)

            for k in range(KT):
                eng.wait_ge(sem("squared"), 56 + k + 1)
                ins = eng.matmul(pj[0][:, 0:S], ones_d[:], SQM[:, k, :], start=(k == 0), stop=(k == KT - 1))
            ins.then_inc(sem("last_ms"), 1)
            eng.wait_ge(sem("r_ready"), 4 * KT)
            for i in range(4):
                for k in range(4):
                    kt = 4 * (i % 2) + k
                    t = i // 2
                    ins = eng.transpose(mi[i][:, k * P:(k + 1) * P], R[:, kt, S + t * P:S + (t + 1) * P], ident[:])
                ins.then_inc(sem("last_turned"), 1)

        @block.scalar
        def _(eng):
            act = Steps(eng, sem("act_steps"))

            def copy(dst, src, func=ACT.Copy, **kw):
                return eng.activation(dst, src, func, **kw)

            def cut_hi(pair, p):
                if isinstance(pair, int) and 2 * pair + p >= DENSE_UNITS:
                    return
                eng.wait_ge(raw_in[p], 32 * (pair + 1))
                if not isinstance(pair, int) or pair > 0:
                    eng.wait_ge(unit_used, 2 * pair + p - 1)
                copy(w_hi[p][:], raw[p][:]).then_inc(hi_done, 1)

            def used(n):
                eng.wait_ge(unit_used, n + 1)

            eng.wait_ge(sem("c_in"), 32)
            copy(csil[:].rearrange("p k s -> p s k"), craw[:], ACT.Silu).then_inc(sem("csil_done"), 1)
            eng.wait_ge(sem("csz_zero"), 1)
            eng.wait_ge(sem("csil_done"), 1)
            copy(csz[:, :, 4:6], csil[:]).then_inc(sem("csz_set"), 1)
            eng.wait_ge(sem("lb_shifted"), 1)
            copy(lbp[:, 2:4, :], lbp[:, 0:2, :], ACT.Exp).then_inc(sem("lb_exp"), 1)
            eng.wait_ge(sem("lb_sum"), 1)
            copy(lbp[:, 5, :], lbp[:, 4, :], ACT.Ln).then_inc(sem("lb_ln"), 1)

            for k in range(ADA_FIRST + 1):
                for p in range(2):
                    cut_hi(k, p)

            def squares(k, n, c0, ready):
                if ready is None:
                    bank, free, full, before = mi_of(("xT", k))
                    eng.wait_ge(free, before + 1)
                else:
                    eng.wait_ge(sem("r_ready"), ready + k)
                copy(SQ[:, k, c0:c0 + n], R[:, k, c0:c0 + n], ACT.Square).then_inc(sem("squared"), 1)

            def inverse_root(name, norm, n):
                bank, free, full, before = mi_of(name)
                eng.wait_ge(mi_full, full)
                if norm > 1:
                    eng.wait_ge(sem("rstd_used"), norm - 1)
                copy(rstd[:, 0:n], bank[:, 0:n], ACT.Ln, bias=eps_t[:]).then_inc(free, 1)
                eng.wait_ge(free, before + 1)
                copy(rstd[:, 0:n], rstd[:, 0:n], ACT.Exp, scale=-0.5).then_inc(sem("rstd_ready"), 1)

            def cut_h_hi(done, c0, n):
                for k in range(KT):
                    eng.wait_ge(sem("h_ready"), done + k + 1)
                    copy(h_hi[:, k, c0:c0 + n], HF[:, k, c0:c0 + n]).then_inc(sem("h_hi_done"), 1)

            def evac(pair, dst, n, func):
                for p in range(2):
                    used(2 * pair + p)
                    for b in (2 * p, 2 * p + 1):
                        x = dst(b)
                        src = pj[b][:, 0:n]
                        if len(x.shape) == 3:
                            src = src.rearrange("p (s t) -> p s t", t=S)
                        copy(x, src, func).then_inc(pj_free[b], 1)
                    cut_hi(pair + 1, p)

            def forget_gates(l, dirs):
                for d in dirs:
                    turn = 2 * l + d + 1
                    if turn > 1:
                        eng.wait_ge(sem("gate_done"), turn - 1)
                        eng.wait_ge(sem("keys_done"), turn - 1)
                    eng.wait_ge(pj_free[3], R_IN[l] + 1 + d)
                    act.step(copy(gE[:], lf[:, d], ACT.Abs))
                    act.step(copy(gE[:], gE[:], ACT.Exp, scale=-1.0))
                    copy(gL[:], gE[:], ACT.Ln, bias=1.0).then_inc(sem("gate_l1"), 1)
                    eng.wait_ge(sem("gate_e"), turn)
                    if l == 0:
                        copy(kk[:, d], gE[:], ACT.Exp, scale=-1.0).then_inc(sem("keys_done"), 1)
                        continue
                    for hd in range(HEADS):
                        ins = copy(kk[:, d, :, hd, :], gE[:, :, hd, :], ACT.Exp, scale=-1.0,
                                   bias=lbp[:, 0, d * 4 + hd:d * 4 + hd + 1])
                        ins.then_inc(*((sem("keys_done"), 1) if hd == HEADS - 1 else (sem("key_heads"), 1)))
                    eng.wait_ge(sem("gate_diff"), d + 1)
                    act.step(copy(gL[:], gE[:], ACT.Abs))
                    act.step(copy(gL[:], gL[:], ACT.Exp, scale=-1.0))
                    copy(gL[:], gL[:], ACT.Ln, bias=1.0).then_inc(sem("gate_l2"), 1)

            last_use = [[], []]

            def gate_tile(l, c, e):
                used(2 * P_IN[l](6 + c) + e // 2)
                n, width = 16 * l + 4 * c + e, NT[l]
                if n:
                    eng.wait_ge(sem("spilled"), 16 * n)
                copy(gate_st[:, 0:width], pj[e][:, 0:width], ACT.Sigmoid).then_inc(pj_free[e], 1)
                eng.wait_ge(pj_free[e], R_IN[l] + 7 + c)
                eng.dma_start(spill[4 * c + e, :, 0:width], gate_st[:, 0:width]).then_inc(sem("spilled"), 16)

            def gates_late(l, c, step):
                if step == 0:
                    cut_hi(P_IN[l](6 + c) + 1, 1)
                else:
                    gate_tile(l, c, 1 + step)

            def decays(l, s, d):
                for li, h in enumerate(LEVELS + [S]):
                    if li < 8 and not FULL[l, s]:
                        continue
                    i = li % 2
                    for w in last_use[i]:
                        eng.wait_ge(*w)
                    eng.wait_ge(sem("ab_ready"), N_EXP[l, s, d, li])
                    if li == 8:
                        if s == 1:
                            copy(QE[0][:], cA[:], ACT.Exp).then_inc(sem("decayed"), 1)
                            last_use[0] = [(sem("q_ready"), N_Q[l, s, d, 8])]
                        else:
                            copy(KE[0][:], cB[:], ACT.Exp).then_inc(sem("decayed"), 1)
                            last_use[0] = [(mi_full, MISC[("kT", l, d, 1)][1])]
                        continue
                    tq, ts = (1, 0) if d == 0 else (0, 1)
                    view = lambda x: x[:].rearrange("p e (b two h) -> p (e b) two h", two=2, h=h)
                    act.mark(copy(view(QE[i])[:, :, tq, :], view(cA)[:, :, tq, :], ACT.Exp))
                    copy(view(KE[i])[:, :, ts, :], view(cB)[:, :, ts, :], ACT.Exp).then_inc(sem("decayed"), 1)
                    last_use[i] = [(mi_full, MISC[("att", l, s, d, li, 1 if h < P else 0)][1])]
                    c = 2 * s + d
                    if li < 3 and c > (2 if l else 0):
                        gates_late(l, c - 1, li)
                    if li == 5:
                        cut_hi(P_IN[l](6 + c) + 1, 0)
                    if li in (5, 6):
                        gate_tile(l, c, li - 5)

            def copy_out(name, dst):
                bank, free, full, before = mi_of(name)
                eng.wait_ge(mi_full, full)
                copy(dst, bank[:].rearrange("p (e n) -> p e n", e=HEADS)).then_inc(free, 1)

            def halves(x, i):
                return x[:, 2 * i:2 * i + 2, :].rearrange("p e t -> p (e t)")

            def head_norm(l, s):
                for i in range(2):
                    bank, free, full, before = mi_of(("o", l, s, i))
                    eng.wait_ge(mi_full, full)
                    copy(halves(cA, i), bank[:], ACT.Square).then_inc(sem("o_squared"), 1)
                for i in range(2):
                    bank, free, full, before = mi_of(("oms", l, s, i))
                    eng.wait_ge(mi_full, full)
                    copy(halves(cB, i), bank[:], ACT.Ln, bias=eps_t[:]).then_inc(free, 1)
                    eng.wait_ge(free, before + 1)
                    copy(halves(cB, i), halves(cB, i), ACT.Exp, scale=-0.5).then_inc(sem("o_rstd"), 1)

            def residual_norm(l, name, norm, ready):
                c0, n = (0, T) if name == "mix_pre" else (C0[l], NT[l])
                for k in range(KT):
                    squares(k, n, c0, ready)
                inverse_root(("ms", l, name), norm, n)

            def evac_out(pair, first_kt, y, sq, c0, n):
                for p in range(2):
                    used(2 * pair + p)
                    for j in range(2):
                        b, kt = 2 * p + j, first_kt + 2 * p + j
                        copy(sq[:, kt, c0:c0 + n], pj[b][:, 0:n], ACT.Square).then_inc(sem("squared"), 1)
                        copy(y[:, kt, c0:c0 + n], pj[b][:, 0:n]).then_inc(pj_free[b], 1)
                    cut_hi(pair + 1, p)

            eng.wait_ge(sem("ones_set"), 3)
            for l in range(2):
                c0, n = C0[l], NT[l]
                residual_norm(l, "mix_pre", 4 * l + 1, None if l == 0 else KT + 1)
                cut_h_hi(2 * KT * l, 0, T)
                if l == 1:
                    eng.wait_ge(sem("lb_ready"), 1)
                dests = [lambda b: lf[:, 0, :, b, :], lambda b: lf[:, 1, :, b, :], lambda b: u[:, b, c0:c0 + n], None,
                         lambda b: g[:, b, c0:c0 + n], lambda b: q[:, c0 // S:2, b, :]]
                funcs = [ACT.Copy, ACT.Copy, ACT.Copy, None, ACT.Silu, ACT.Silu]
                for i in range(6):
                    pair = P_IN[l](i)
                    if l == 0:
                        for p in range(2):
                            cut_hi(pair, p)
                    if 1 <= i <= 2:
                        forget_gates(l, [i - 1])
                    if i == 3:
                        for p in range(2):
                            used(2 * pair + p)
                            if p == 1:
                                for t in range(4):
                                    copy(v[:, t, :], pj[t][:]).then_inc(pj_free[t], 1)
                            cut_hi(pair + 1, p)
                    else:
                        evac(pair, dests[i], T if i < 2 else n, funcs[i])
                last_use[0] = last_use[1] = [(sem("gate_done"), 2 * l + 2), (sem("keys_done"), 2 * l + 2)]
                for s in range(2):
                    if FULL[l, s]:
                        last_use[1] = [(mi_full, MISC[("diag", l, s, 1)][1])]
                        last_use[0] = last_use[0] + [(sem("diag_q"), 1 + s + l), (sem("diag_k"), 1 + s + l)]
                    for d in range(2):
                        decays(l, s, d)
                        if s == 0:
                            for t in range(2):
                                copy_out(("kT", l, d, t), kept_keys(d)[:, t])
                            copy_out(("st", l, d), state[:, d])
                        if not FULL[l, s]:
                            for p in range(2):
                                for e in (2 * p, 2 * p + 1):
                                    gate_tile(l, d, e)
                                cut_hi(P_IN[l](6 + d) + 1, p)
                    if FULL[l, s]:
                        head_norm(l, s)
                for step in range(3):
                    gates_late(l, 3, step)
                used(2 * P_IN[l](9) + 1)
                eng.wait_ge(sem("y_rec"), (2, 3)[l])
                for src, hi in ((g, yr_hi), (u, yp_hi)):
                    for i in range(2):
                        copy(hi[:, 2 * i:2 * i + 2, c0:c0 + n], src[:, 2 * i:2 * i + 2, c0:c0 + n])\
                            .then_inc(sem("branch_hi"), 1)
                for b in range(N_BR):
                    for j in range(2):
                        eng.wait_ge(sem("m_ready"), 8 * l + 2 * b + j + 1)
                        copy(m_hi[:, 2 * b + j, c0:c0 + n], mt[2 * j][:, 0:n]).then_inc(sem("m_hi_done"), 1)
                    cut_hi(P_BR[l] + b // 2 + 1, b % 2)
                for i in range(2):
                    if l == 0:
                        for p in range(2):
                            cut_hi(P_OUT[0](i), p)
                    evac_out(P_OUT[l](i), 4 * i, Y, SQ, c0, n)
                inverse_root(("ms", l, "mix_post"), 4 * l + 2, n)
                residual_norm(l, "ffn_pre", 4 * l + 3, 2 * KT * l + 1)
                if l == 0:
                    cut_h_hi(KT, 0, T)
                    with eng.Fori(0, N_GU // 2) as i:
                        pair = P_GU(i)
                        for p in range(2):
                            cut_hi(pair, p)
                        used(2 * pair)
                        for j in range(2):
                            eng.wait_ge(pj_free[2 + j], R_GU + i)
                            copy(sg[:, j, :], pj[j][:], ACT.Silu).then_inc(pj_free[j], 1)
                        cut_hi(pair + 1, 0)
                        cut_hi(pair + 1, 1)
                        for j in range(2):
                            eng.wait_ge(pj_free[2 + j], R_GU + i + 1)
                            copy(hid_hi[:, bass.ds(2 * i + j, 1), :].rearrange("p a n -> p (a n)"), hf[:, j, :])\
                                .then_inc(sem("hid_hi_done"), 1)
                    for p in range(2):
                        cut_hi(P_DN, p)
                    for gr in range(4):
                        for pc in range(3):
                            used(2 * P_DN + 3 * gr + pc)
                            if pc == 2:
                                for j in range(2):
                                    b, kt = 2 * (gr % 2) + j, 2 * gr + j
                                    copy(SQ2[:, kt, :], pj[b][:], ACT.Square).then_inc(sem("squared"), 1)
                                    copy(Y2[:, kt, :], pj[b][:]).then_inc(pj_free[b], 1)
                            nxt = 2 * P_DN + 3 * gr + pc + 2
                            cut_hi(nxt // 2, nxt % 2)
                    inverse_root(("ms", l, "ffn_post"), 4, T)

            eng.wait_ge(sem("top_diff"), 1)
            copy(tmp1[:, 2:4], tmp1[:, 0:2], ACT.Exp).then_inc(sem("top_exp"), 1)
            for i in range(4):
                bank, free, full, before = mi_of(("h2", i))
                eng.wait_ge(mi_full, full)
                copy(h2_hi[:, i // 2, (i % 2) * 512:(i % 2 + 1) * 512], bank[:]).then_inc(sem("h2_hi_done"), 1)
            copy(scat[:, 0, :], HM[:, 0, :], scale=0.0).then_inc(sem("scat_first"), 1)
            for j in range(JOBS):
                bank, free, full, before = mi_of(("pT", j))
                eng.wait_ge(mi_full, full)
                copy(scat[:, j + 1, :], bank[:, 0:S]).then_inc(free, 1)
            eng.wait_ge(sem("jobs_ready"), 1)
            n_jobs = eng.value_load(jobs[0:1, 0:1], min_val=NE, max_val=JOBS)

            def gathered_hi(j):
                for half in range(2):
                    eng.wait_ge(sem("gathered"), 4 * j + half + 1)
                    copy(xg_hi[:, 4 * half:4 * half + 4, :].rearrange("p k n -> p (k n)"), mi[2 + half][:])\
                        .then_inc(sem("xg_hi_done"), 1)

            def scaled_hi(j):
                for half in range(2):
                    copy(ye_hi[:, half * 512:(half + 1) * 512], pj[2 + half][:],
                         scale=gslot[:, bass.ds(j, 1)]).then_inc(sem("ye_hi_done"), 1)

            gathered_hi(0)
            with eng.Fori(0, n_jobs) as j:
                def cut_job_hi(n):
                    eng.wait_ge(rawm_in[n % RAW_M], (JU // RAW_M * 32) * j + 32 * (n // RAW_M + 1))
                    eng.wait_ge(unit_used, DENSE_UNITS + j * JU + n - HL_M + 1)
                    copy(mw_hi[n % HL_M][:], raw_m[n % RAW_M][:]).then_inc(hi_done, 1)

                def turned_hi(st):
                    eng.wait_ge(sem("turned"), j * STEPS + st + 1)
                    copy(ht_hi[st % 2][:].rearrange("p a n -> p (a n)"), mi[st % 2][:, 0:256])\
                        .then_inc(sem("ht_hi_done"), 1)

                for n in range(HL_M):
                    cut_job_hi(n)
                scaled_hi(j)
                for n, (kind, st) in enumerate(ORDER):
                    if kind == "B":
                        eng.wait_ge(unit_used, DENSE_UNITS + j * JU + n + 1)
                        if st >= 2:
                            eng.wait_ge(sem("he_done"), j * STEPS + st - 1)
                        copy(sge[st % 2][:], pj[st % 2][:, 0:256], ACT.Silu).then_inc(sem("sge_done"), 1)
                    if n + HL_M < JU:
                        cut_job_hi(n + HL_M)
                    if kind == "B" and st >= 1:
                        turned_hi(st - 1)
                    if (kind, st) == ("B", STEPS - 1):
                        gathered_hi(j + 1)
                    if (kind, st) == ("D", STEPS - 3):
                        turned_hi(STEPS - 1)
            eng.wait_ge(unit_used, n_jobs * JU + DENSE_UNITS)
            scaled_hi(n_jobs)
            eng.wait_ge(sem("acc_done"), n_jobs * 4 + 8)
            for k in range(KT):
                copy(SQM[:, k, :], acc[:, k, :], ACT.Square).then_inc(sem("squared"), 1)
            eng.wait_ge(sem("last_ms"), 1)
            act.step(copy(rstd[:, 0:S], pj[0][:, 0:S], ACT.Ln, bias=eps_t[:]))
            copy(rstd[:, 0:S], rstd[:, 0:S], ACT.Exp, scale=-0.5).then_inc(sem("rstd_ready"), 1)

        @block.vector
        def _(eng):
            dve = Steps(eng, sem("dve_steps"))
            tt, ts_, stt = eng.tensor_tensor, eng.tensor_scalar, eng.scalar_tensor_tensor

            def cut_lo(pair, p):
                if isinstance(pair, int) and 2 * pair + p >= DENSE_UNITS:
                    return
                eng.wait_ge(hi_done, 2 * pair + p + 1)
                k = slice(0, VK)
                tt(w_lo[p][:, k, :], raw[p][:, k, :], w_hi[p][:, k, :], ALU.subtract).then_inc(lo_dve, 1)

            def full_tile(name):
                bank, free, full, before = mi_of(name)
                eng.wait_ge(mi_full, full)
                return bank, free

            eng.memset(ones_d[:], 1.0 / D).then_inc(sem("ones_set"), 1)
            eng.memset(ones_h[:], 1.0 / P).then_inc(sem("ones_set"), 1)
            eng.memset(eps_t[:], EPS).then_inc(sem("ones_set"), 1)
            dve.step(eng.memset(Y[:, 0, 0:KT * 12], 0.0))
            eng.tensor_copy(csz[:].rearrange("p k n -> p (k n)"), Y[:, 0, 0:KT * 12]).then_inc(sem("csz_zero"), 1)
            eng.wait_ge(sem("csz_set"), 1)
            tt(csz[:, :, 6:8], csil[:], csz[:, :, 4:6], ALU.subtract).then_inc(sem("csz_set"), 1)
            for k in range(KT):
                bank, free = full_tile(("xT", k))
                eng.tensor_copy(R[:, k, :], bank[:]).then_inc(free, 1)
            bank, free = full_tile("prmA")
            eng.tensor_copy(adab[:], bank[:, 0:96]).then_inc(free, 1)
            bank, free = full_tile("prmB")
            eng.tensor_copy(prm[:], bank[:, 0:96]).then_inc(free, 1)
            eng.wait_ge(free, MISC["prmB"][2] + 1)
            eng.wait_ge(sem("consts_in"), 48)
            eng.tensor_copy(masks[:], masks_f[:]).then_inc(sem("masks_set"), 1)
            dve.step(tt(lbp[:, 4, :], prm[:, 64:72], prm[:, 72:80], ALU.max))
            dve.mark(tt(lbp[:, 0, :], prm[:, 64:72], lbp[:, 4, :], ALU.subtract))
            tt(lbp[:, 1, :], prm[:, 72:80], lbp[:, 4, :], ALU.subtract).then_inc(sem("lb_shifted"), 1)
            eng.wait_ge(sem("lb_exp"), 1)
            tt(lbp[:, 4, :], lbp[:, 2, :], lbp[:, 3, :], ALU.add).then_inc(sem("lb_sum"), 1)
            eng.wait_ge(sem("lb_ln"), 1)
            dve.mark(tt(lbp[:, 0, :], lbp[:, 0, :], lbp[:, 5, :], ALU.subtract))
            tt(lbp[:, 1, :], lbp[:, 1, :], lbp[:, 5, :], ALU.subtract).then_inc(sem("lb_ready"), 1)
            flat = mod[:].rearrange("p l c s -> p (l c s)")

            def ada_rows(k, i=0):
                b, full, _ = MISC[("rows", k)]
                eng.wait_ge(unit_used, ADA_USED(k, i))
                eng.tensor_copy(rows_sb[:], mi[b][0:8, 0:UC]).then_inc(mi_free[b], 1)

            def ada_mod(k, i=0):
                b, full, _ = MISC[("mod", k)]
                eng.wait_ge(mi_full, full + i)
                eng.tensor_copy(flat[:, bass.ds(8 * (k + i), 8)], mi[b][:, 0:8]).then_inc(mi_free[b], 1)

            def finish(l, chunks):
                eng.wait_ge(mi_free[1], MISC[("mod", 4 * (3 * l + max(chunks) // 2) + 3)][2] + 1)
                bias = adab[:].rearrange("p (l c s) -> p l c s", l=2, s=1).to_broadcast([P, 2, 48, 2])
                first, last = 8 * min(chunks), 8 * max(chunks) + 8
                dve.step(tt(mod[:, l, first:last], mod[:, l, first:last], bias[:, l, first:last], ALU.add))
                for chunk, row, plus in ((1, 0, 1.0), (4, 32, 1.0), (2, 16, 0.0), (5, 48, 0.0)):
                    if chunk in chunks:
                        m = mod[:, l, 8 * chunk:8 * chunk + 8, :]
                        w = prm[:, row + 8 * l:row + 8 * l + 8].rearrange("p (c s) -> p c s", s=1)
                        dve.mark(stt(m, m, plus, w.to_broadcast([P, 8, 2]), ALU.add, ALU.mult))
                dve.sync()

            def column(l, chunk, k, s):
                return mod[:, l, 8 * chunk + k, s:s + 1]

            def streams(l, name):
                return (0, 1) if l == 0 or name == "mix_pre" else (1,)

            def modulate(l, name, norm, dst, d0, signal, done=None):
                chunk = 0 if name == "mix_pre" else 3
                eng.wait_ge(sem("rstd_ready"), norm)
                sts = streams(l, name)
                c0, n = sts[0] * S, len(sts) * S
                for k in range(KT):
                    ins = tt(dst[:, k, c0 - d0:c0 - d0 + n], R[:, k, c0:c0 + n], rstd[:, 0:n], ALU.mult)
                    ins.then_inc(*((sem("rstd_used"), 1) if k == KT - 1 else (dve.sem, 1)))
                    dve.k += k < KT - 1
                eng.wait_ge(sem("rstd_used"), norm)
                for k in range(KT):
                    for s in sts:
                        x = dst[:, k, s * S - d0:(s + 1) * S - d0]
                        ins = ts_(x, x, column(l, chunk + 1, k, s), column(l, chunk, k, s), ALU.mult, ALU.add)
                        ins.then_inc(*((signal, 1) if s == sts[-1] else (dve.sem, 1)))
                        dve.k += s != sts[-1]
                    if done is not None and k >= 2:
                        cut_h_lo(done, 0, T, [k - 2])
                if done is not None:
                    cut_h_lo(done, 0, T, [KT - 2, KT - 1])

            def cut_h_lo(done, c0, n, tiles):
                for k in tiles:
                    eng.wait_ge(sem("h_hi_done"), done + k + 1)
                    tt(h_lo[:, k, c0:c0 + n], HF[:, k, c0:c0 + n], h_hi[:, k, c0:c0 + n], ALU.subtract)\
                        .then_inc(sem("h_cut"), 1)

            def add_branch(l, chunk, norm, y, c0, n, y0=0):
                eng.wait_ge(sem("rstd_ready"), norm)
                for k in range(KT):
                    yk = y[:, k, c0 - y0:c0 - y0 + n]
                    ins = tt(yk, yk, rstd[:, 0:n], ALU.mult)
                    ins.then_inc(*((sem("rstd_used"), 1) if k == KT - 1 else (dve.sem, 1)))
                    dve.k += k < KT - 1
                eng.wait_ge(sem("rstd_used"), norm)
                for k in range(KT):
                    for s in ((0, 1) if n == T else (1,)):
                        r = R[:, k, s * S:(s + 1) * S]
                        ins = stt(r, y[:, k, s * S - y0:(s + 1) * S - y0], column(l, chunk, k, s), r, ALU.mult, ALU.add)
                        ins.then_inc(*((sem("r_ready"), 1) if s == 1 else (dve.sem, 1)))
                        dve.k += s != 1

            def merged(x):
                return x.rearrange("p s e t -> p (s e t)")

            def forget_gates(l, dirs):
                for d in dirs:
                    turn = 2 * l + d + 1
                    z = merged(lf[:, d])
                    eng.wait_ge(sem("gate_l1"), turn)
                    stt(merged(gE[:]), z, 0.0, merged(gL[:]), ALU.max, ALU.add).then_inc(sem("gate_e"), 1)
                    eng.wait_ge(sem("gate_e"), turn)
                    ins = stt(z, z, 0.0, merged(gL[:]), ALU.min, ALU.subtract)
                    if l == 0:
                        ins.then_inc(sem("gate_done"), 1)
                        continue
                    dve.step(ins)
                    for hd in range(HEADS):
                        x = lf[:, d, :, hd, :]
                        dve.mark(ts_(x, x, lbp[:, 0, d * 4 + hd:d * 4 + hd + 1], None, ALU.add))
                    dve.sync()
                    eng.wait_ge(sem("keys_done"), turn)
                    for hd in range(HEADS):
                        ins = ts_(gE[:, :, hd, :], lf[:, d, :, hd, :], lbp[:, 1, d * 4 + hd:d * 4 + hd + 1],
                                  None, ALU.subtract)
                        if hd < HEADS - 1:
                            dve.mark(ins)
                    ins.then_inc(sem("gate_diff"), 1)
                    eng.wait_ge(sem("gate_diff"), d + 1)
                    for hd in range(HEADS):
                        x = lf[:, d, :, hd, :]
                        dve.mark(ts_(x, x, lbp[:, 1, d * 4 + hd:d * 4 + hd + 1], None, ALU.max))
                    dve.sync()
                    eng.wait_ge(sem("gate_l2"), d + 1)
                    tt(z, z, merged(gL[:]), ALU.add).then_inc(sem("gate_done"), 1)

            taken = [None, None]

            def take(name, t, dst, mask=None):
                bank, free = full_tile(name)
                if taken[t]:
                    eng.wait_ge(*taken[t])
                src = bank[:].rearrange("p (e n) -> p e n", e=HEADS)
                if mask is None:
                    eng.tensor_copy(dst, src).then_inc(free, 1)
                else:
                    eng.copy_predicated(dst, mask, src).then_inc(free, 1)
                taken[t] = (free, MISC[name][2] + 1)

            def take_products(l, s, d, li):
                if LEVELS[li] == P:
                    st, qt = (0, 1) if d == 0 else (1, 0)
                    take(("att", l, s, d, li, 0), st, att[:, st, :, qt * P:(qt + 1) * P])
                    return
                mask = masks[:, 7 * d + li:7 * d + li + 1, :].to_broadcast([P, HEADS, P])
                for t in range(2):
                    take(("att", l, s, d, li, t), t, att[:, t, :, t * P:(t + 1) * P], mask)

            def halves_of(x, h):
                return x.rearrange("p e (b two h) -> p (e b) two h", two=2, h=h)

            def scan(l, s, d):
                n = SCANS.index((l, s, d))
                if n:
                    eng.wait_ge(sem("decayed"), N_EXP[SCANS[n - 1] + (8,)])
                dve.mark(eng.tensor_copy(cA[:], lf[:, d, s]))
                ins = eng.memset(cB[:], 0.0)
                if FULL[l, s]:
                    ins.then_inc(sem("ab_ready"), 1)
                    eng.wait_ge(sem("ab_ready"), N_EXP[l, s, d, 0])
                else:
                    dve.step(ins)
                tq, tk = (1, 0) if d == 0 else (0, 1)
                for li, h in enumerate(LEVELS):
                    if FULL[l, s]:
                        eng.wait_ge(sem("decayed"), N_EXP[l, s, d, li])
                        x = halves_of(QE[li % 2][:], h)[:, :, tq, :]
                        stt(x, x, HS, halves_of(q[:, s], h)[:, :, tq, :], ALU.mult, ALU.mult)\
                            .then_inc(sem("q_ready"), 1)
                    a_, b_ = halves_of(cA[:], h), halves_of(cB[:], h)
                    edge = h - 1 if d == 0 else 0
                    half = [P, a_.shape[1], h]
                    dve.step(tt(b_[:, :, tk, :], b_[:, :, tk, :], a_[:, :, tq, edge:edge + 1].to_broadcast(half),
                                ALU.add))
                    ins = tt(a_[:, :, tq, :], a_[:, :, tq, :], a_[:, :, tk, edge:edge + 1].to_broadcast(half), ALU.add)
                    if FULL[l, s] or li == 7:
                        ins.then_inc(sem("ab_ready"), 1)
                        nxt = N_EXP[l, s, d, li + 1]
                        eng.wait_ge(sem("ab_ready"), nxt)
                    else:
                        dve.step(ins)
                    if FULL[l, s] and li == 0 and d == 0:
                        for t in range(2):
                            take(("diag", l, s, t), t, att[:, t, :, t * P:(t + 1) * P])
                    if FULL[l, s] and li >= 1:
                        take_products(l, s, d, li - 1)
                    c = 2 * s + d
                    if FULL[l, s] and li == 2 and c > (2 if l else 0):
                        cut_lo(P_IN[l](5 + c) + 1, 1)
                    if FULL[l, s] and li == 6:
                        cut_lo(P_IN[l](6 + c) + 1, 0)
                if FULL[l, s]:
                    take_products(l, s, d, 7)
                if s == 1:
                    eng.wait_ge(sem("decayed"), N_EXP[l, s, d, 8])
                    stt(lf[:, d, 1], QE[0][:], HS, q[:, 1], ALU.mult, ALU.mult).then_inc(sem("q_ready"), 1)

            def head_norm(l, s, turn):
                for i in range(2):
                    bank, free, full, before = mi_of(("o", l, s, i))
                    eng.wait_ge(sem("o_rstd"), 2 * turn + i + 1)
                    x = slice(2 * i, 2 * i + 2)
                    tt(cA[:, x, :], bank[:].rearrange("p (e n) -> p e n", e=2), cB[:, x, :], ALU.mult).then_inc(free, 1)
                    eng.wait_ge(free, before + 1)
                for hd in range(HEADS):
                    y = g[:, hd, s * S:(s + 1) * S]
                    ins = stt(y, cA[:, hd, :], prm[:, 80 + 4 * l + hd:81 + 4 * l + hd], y, ALU.mult, ALU.mult)
                    if hd < HEADS - 1:
                        dve.mark(ins)
                ins.then_inc(sem("y_rec"), 1)

            def cut_pairs(first, last):
                with eng.Fori(first, last) as i:
                    for p in range(2):
                        cut_lo(i, p)

            for p in range(2):
                cut_lo(0, p)
            for k in range(ADA_FIRST):
                for p in range(2):
                    cut_lo(k + 1, p)
                ada_rows(k)
                ada_mod(k)
            finish(0, (0, 1))
            turn = 0
            for l in range(2):
                c0, n = C0[l], NT[l]
                modulate(l, "mix_pre", 4 * l + 1, HF, 0, sem("h_ready"), 2 * KT * l)
                for i in range(6):
                    pair = P_IN[l](i)
                    if l == 0:
                        for p in range(2):
                            cut_lo(pair, p)
                    if l == 0:
                        ada_rows(ADA_FIRST + i)
                    if 1 <= i <= 2:
                        forget_gates(l, [i - 1])
                    cut_lo(pair + 1, 0)
                    if l == 0:
                        ada_mod(ADA_FIRST + i)
                    cut_lo(pair + 1, 1)
                eng.wait_ge(pj_free[3], R_IN[l] + 6)
                for gi in range(4):
                    bank, free = full_tile(("pool", l, gi))
                    ts_(u[:, gi, c0:c0 + n], bank[:, 0:n], prm[:, 88 + 4 * l + gi:89 + 4 * l + gi], None, ALU.mult)\
                        .then_inc(free, 1)
                if l == 0:
                    eng.wait_ge(sem("masks_set"), 1)
                eng.wait_ge(sem("keys_done"), 2 * l + 2)
                eng.wait_ge(sem("gate_done"), 2 * l + 2)
                for s in range(2):
                    if FULL[l, s]:
                        if (l, s) == (0, 1):
                            eng.wait_ge(mi_full, MISC[("att", 0, 0, 1, 7, 0)][1])
                        if (l, s) != (0, 1):
                            dve.mark(eng.memset(QE[0][:], 0.0))
                        ts_(QE[1][:], q[:, s], HS, None, ALU.mult).then_inc(sem("diag_q"), 1)
                    for d in range(2):
                        scan(l, s, d)
                        if not FULL[l, s]:
                            for p in range(2):
                                cut_lo(P_IN[l](6 + d) + 1, p)
                    if FULL[l, s]:
                        head_norm(l, s, turn)
                        eng.wait_ge(sem("y_rec"), turn + 1)
                        turn += 1
                cut_lo(P_BR[l], 1)
                for i, (src, hi, lo) in enumerate(((g, yr_hi, yr_lo), (u, yp_hi, yp_lo))):
                    for j in range(2):
                        eng.wait_ge(sem("branch_hi"), 4 * l + 2 * i + j + 1)
                        x = (slice(None), slice(2 * j, 2 * j + 2), slice(c0, c0 + n))
                        tt(lo[x], src[x], hi[x], ALU.subtract).then_inc(sem("branches_cut"), 1)
                for b in range(N_BR):
                    eng.wait_ge(unit_used, 2 * P_BR[l] + b + 1)
                    eng.wait_ge(sem(f"gates_in{b % 2}"), 32 * (2 * l + b // 2 + 1))
                    if b:
                        eng.wait_ge(sem("m_cut"), 8 * l + 2 * b)
                    for j in range(2):
                        for i in range(2):
                            tt(mt[2 * j + i][:, 0:n], sgate[b % 2][:, i, j, 0:n], pj[2 * i + j][:, 0:n], ALU.mult)\
                                .then_inc(pj_free[2 * i + j], 1)
                        for i in range(2):
                            eng.wait_ge(pj_free[2 * i + j], R_BR[l] + b + 1)
                        tt(mt[2 * j][:, 0:n], mt[2 * j][:, 0:n], mt[2 * j + 1][:, 0:n], ALU.add)\
                            .then_inc(sem("m_ready"), 1)
                    for j in range(2):
                        kt = 2 * b + j
                        eng.wait_ge(sem("m_hi_done"), 8 * l + kt + 1)
                        tt(m_lo[:, kt, c0:c0 + n], mt[2 * j][:, 0:n], m_hi[:, kt, c0:c0 + n], ALU.subtract)\
                            .then_inc(sem("m_cut"), 1)
                    cut_lo(P_BR[l] + b // 2 + 1, b % 2)
                for i in range(N_OUT // 2):
                    if l == 0:
                        for p in range(2):
                            cut_lo(P_OUT[0](i), p)
                        ada_rows(ADA_FIRST + 6 + i)
                    for p in range(2):
                        cut_lo(P_OUT[l](i) + 1, p)
                        if l == 0 and p == 0:
                            ada_mod(ADA_FIRST + 6 + i)
                if l == 0:
                    finish(0, (2, 3, 4, 5))
                add_branch(l, 2, 4 * l + 2, Y, c0, n)
                if l == 1:
                    modulate(1, "ffn_pre", 7, HM, S, sem("hm_ready"))
                    continue
                modulate(0, "ffn_pre", 3, HF, 0, sem("h_ready"), KT)
                with eng.Fori(0, N_GU // 2) as i:
                    pair = P_GU(i)
                    for p in range(2):
                        cut_lo(pair, p)
                    ada_rows(ADA_FIRST + 8, i)
                    cut_lo(pair + 1, 0)
                    ada_mod(ADA_FIRST + 8, i)
                    eng.wait_ge(unit_used, 2 * pair + 2)
                    eng.wait_ge(lo_dve, 2 * pair + 3)
                    for j in range(2):
                        eng.wait_ge(pj_free[j], R_GU + i + 1)
                        tt(hf[:, j, :], sg[:, j, :], pj[2 + j][:], ALU.mult).then_inc(pj_free[2 + j], 1)
                    cut_lo(pair + 1, 1)
                    for j in range(2):
                        eng.wait_ge(sem("hid_hi_done"), 2 * i + j + 1)
                        kt = bass.ds(2 * i + j, 1)
                        tt(hid_lo[:, kt, :], hf[:, j:j + 1, :], hid_hi[:, kt, :], ALU.subtract)\
                            .then_inc(sem("hid_cut"), 1)
                for p in range(2):
                    cut_lo(P_DN, p)
                ada_rows(N_ADA - 1)
                ada_mod(N_ADA - 1)
                cut_pairs(P_DN + 1, P_DN + 7)
                finish(1, (0, 1, 2, 3, 4, 5))
                add_branch(0, 5, 4, Y2, 0, T)

            dve.mark(eng.memset(ones_1[:], 1.0))
            dve.mark(eng.memset(gslot[:, 0:1], 0.0))
            dve.step(eng.memset(keys[:], -1.0))
            for t in range(2):
                bank, free = full_tile(("logit", t))
                eng.tensor_copy(lg[:, t, :], bank[:, 0:NE]).then_inc(free, 1)
                eng.wait_ge(free, MISC[("logit", t)][2] + 1)
                dve.step(eng.max(top_v[:, t, :], lg[:, t, :]))
                dve.step(eng.max_index(top_i[:, t, :], top_v[:, t, :], lg[:, t, :]))
            dve.step(eng.tensor_copy(top_f[:], top_i[:]))
            eng.wait_ge(sem("route_in"), 48)
            for t in range(2):
                for k in range(2):
                    dve.mark(ts_(tmp8[:, 2 * t + k, :], iota[:, 0:NE], top_f[:, t, k:k + 1], None, ALU.is_equal))
            dve.sync()
            tt(tmp1[:, 0:2].rearrange("p (t a) -> p t a", a=1), top_v[:, :, 1:2], top_v[:, :, 0:1], ALU.subtract)\
                .then_inc(sem("top_diff"), 1)
            for t in range(2):
                ins = tt(sel[:, t, :], tmp8[:, 2 * t, :], tmp8[:, 2 * t + 1, :], ALU.add)
                ins.then_inc(*((sem("sel_ready"), 1) if t else (dve.sem, 1)))
                dve.k += 1 - t
            eng.wait_ge(sem("top_exp"), 1)
            dve.step(ts_(tmp1[:, 4:6], tmp1[:, 2:4], 1.0, None, ALU.add))
            dve.step(eng.reciprocal(tmp1[:, 4:6], tmp1[:, 4:6]))
            dve.step(tt(tmp1[:, 6:8], tmp1[:, 2:4], tmp1[:, 4:6], ALU.mult))
            for t in range(2):
                dve.mark(ts_(gates[:, t, 0:NE], tmp8[:, 2 * t, :], tmp1[:, 4 + t:5 + t], None, ALU.mult))
            dve.sync()
            for t in range(2):
                dve.mark(stt(gates[:, t, 0:NE], tmp8[:, 2 * t + 1, :], tmp1[:, 6 + t:7 + t], gates[:, t, 0:NE],
                             ALU.mult, ALU.add))
            for i in range(4):
                eng.memset(acc[:, 2 * i:2 * i + 2, :], 0.0).then_inc(sem("acc_done"), 1)
            for i in range(4):
                bank, free = full_tile(("h2", i))
                eng.wait_ge(sem("h2_hi_done"), i + 1)
                x = (slice(None), i // 2, slice((i % 2) * 512, (i % 2 + 1) * 512))
                tt(h2_lo[x], bank[:], h2_hi[x], ALU.subtract).then_inc(free, 1)
            bank, free = full_tile("rank")
            for t in range(2):
                dve.mark(stt(keys[:, t, 0:NE], bank[:, 8 * t:8 * t + 8], 1.0, sel[:, t, :], ALU.add, ALU.mult))
            dve.sync()
            for t in range(2):
                dve.mark(ts_(keys[:, t, 0:NE], keys[:, t, 0:NE], 1.0, None, ALU.subtract))
            eng.tensor_single_scalar(tmp8[:, 0, :], bank[:, 16:24], float(P), ALU.is_gt).then_inc(free, 1)
            eng.wait_ge(free, MISC["rank"][2] + 1)
            dve.step(eng.tensor_copy(tmp8[:, 1, :], tmp8[:, 0, :]))
            a_, b_ = 1, 2
            for sh in (1, 2, 4):
                dve.mark(eng.tensor_copy(tmp8[:, b_, 0:sh], tmp8[:, a_, 0:sh]))
                dve.step(tt(tmp8[:, b_, sh:NE], tmp8[:, a_, sh:NE], tmp8[:, a_, 0:NE - sh], ALU.add))
                a_, b_ = b_, a_
            dve.mark(ts_(jobs_f[:, 0:1], tmp8[:, a_, NE - 1:NE], float(NE), None, ALU.add))
            dve.step(tt(tmp8[:, 3, :], tmp8[:, a_, :], tmp8[:, 0, :], ALU.subtract))
            dve.mark(eng.tensor_copy(jobs_f[:, 1:1 + NE], iota[:, 0:NE]))
            for r in range(JOBS - NE):
                dve.step(stt(tmp8[:, 4, :], tmp8[:, 3, :], float(r), tmp8[:, 0, :], ALU.is_equal, ALU.mult))
                for i, (x, minus, dst) in enumerate(((keys[:, 0, 0:NE], float(P), keys[:, 0, NE + r:NE + r + 1]),
                                                     (keys[:, 1, 0:NE], float(P), keys[:, 1, NE + r:NE + r + 1]),
                                                     (gates[:, 0, 0:NE], 0.0, gates[:, 0, NE + r:NE + r + 1]),
                                                     (gates[:, 1, 0:NE], 0.0, gates[:, 1, NE + r:NE + r + 1]),
                                                     (iota[:, 0:NE], 0.0, jobs_f[:, 1 + NE + r:2 + NE + r]))):
                    dve.step(stt(tmp8[:, 5, :], x, minus, tmp8[:, 4, :], ALU.subtract, ALU.mult))
                    dve.step(eng.tensor_reduce(dst, tmp8[:, 5, :], AX.X, ALU.add))
            eng.tensor_copy(jobs[:, 0:12], jobs_f[:]).then_inc(sem("jobs_ready"), 1)
            for t in range(2):
                for j in range(JOBS + 1):
                    ins = ts_(one_hot[:, t, j, :], iota[:], keys[:, t, j:j + 1], None, ALU.is_equal)
                    if (t, j) != (1, JOBS):
                        dve.mark(ins)
            ins.then_inc(sem("one_hot_ready"), 1)
            bank, free = full_tile("gslot")
            eng.tensor_copy(gslot[:, 1:1 + JOBS], bank[:, 0:JOBS]).then_inc(free, 1)

            eng.wait_ge(sem("jobs_ready"), 1)
            n_jobs = eng.value_load(jobs[0:1, 0:1], min_val=NE, max_val=JOBS)

            def gathered_lo(j):
                for half in range(2):
                    eng.wait_ge(sem("gathered"), 4 * j + half + 3)
                    eng.tensor_copy(xg_lo[:, 4 * half:4 * half + 4, :].rearrange("p k n -> p (k n)"), mi[2 + half][:])\
                        .then_inc(sem("xg_cut"), 1)

            def scaled_lo(j):
                for half in range(2):
                    eng.wait_ge(sem("ye_hi_done"), 2 * j + half + 1)
                    x = slice(half * 512, (half + 1) * 512)
                    stt(ye_lo[:, x], pj[2 + half][:], gslot[:, bass.ds(j, 1)], ye_hi[:, x], ALU.mult, ALU.subtract)\
                        .then_inc(sem("ye_lo_done"), 1)

            def add_rows(j, r):
                eng.wait_ge(sem("scattered"), 4 * j + r + 1)
                x = acc[:, 2 * r:2 * r + 2, :].rearrange("p k n -> p (k n)")
                tt(x, x, mi[2 + r % 2][:], ALU.add).then_inc(sem("acc_done"), 1)

            gathered_lo(0)
            with eng.Fori(0, n_jobs) as j:
                def cut_job_lo(n):
                    eng.wait_ge(hi_done, DENSE_UNITS + j * JU + n + 1)
                    x = (slice(None), slice(0, VM))
                    tt(mw_lo[n % HL_M][x], raw_m[n % RAW_M][x], mw_hi[n % HL_M][x], ALU.subtract).then_inc(lo_dve, 1)

                def turned_lo(st):
                    eng.wait_ge(sem("ht_hi_done"), j * STEPS + st + 1)
                    tt(ht_lo[st % 2][:].rearrange("p a n -> p (a n)"), mi[st % 2][:, 0:256],
                       ht_hi[st % 2][:].rearrange("p a n -> p (a n)"), ALU.subtract).then_inc(sem("ht_lo_done"), 1)

                for n in range(HL_M):
                    cut_job_lo(n)
                scaled_lo(j)
                for n, (kind, st) in enumerate(ORDER):
                    if kind == "B":
                        eng.wait_ge(sem("sge_done"), j * STEPS + st + 1)
                        tt(he[st % 2][:], sge[st % 2][:], pj[st % 2][:, 256:512], ALU.mult).then_inc(sem("he_done"), 1)
                    if n + HL_M < JU:
                        cut_job_lo(n + HL_M)
                    if kind == "B" and st >= 1:
                        turned_lo(st - 1)
                    if kind == "B" and st <= 1:
                        add_rows(j, 2 * st)
                        add_rows(j, 2 * st + 1)
                    if (kind, st) == ("D", STEPS - 3):
                        gathered_lo(j + 1)
                        turned_lo(STEPS - 1)
            scaled_lo(n_jobs)
            for r in range(4):
                add_rows(n_jobs, r)

            add_branch(1, 5, 8, acc, S, S, y0=S)
            for i in range(4):
                eng.wait_ge(sem("last_turned"), i + 1)
                eng.tensor_copy(fin[:, i // 2, (i % 2) * 512:(i % 2 + 1) * 512], mi[i][:]).then_inc(sem("fin_done"), 1)

        @block.gpsimd
        def _(eng):
            pool = Steps(eng, sem("pool_steps"))
            tt = eng.tensor_tensor

            def cut_lo(pair, p):
                eng.wait_ge(hi_done, 2 * pair + p + 1)
                k = slice(VK, KT)
                tt(w_lo[p][:, k, :], raw[p][:, k, :], w_hi[p][:, k, :], ALU.subtract).then_inc(lo_pool, 1)

            def cut_pairs(first, last):
                with eng.Fori(first, last) as i:
                    for p in range(2):
                        cut_lo(i, p)

            def pooling(l):
                eng.wait_ge(sem("h_cut"), 8 * (2 * l + 1))
                eng.dma_start(invc[:], A["k_invc"]).then_inc(sem("invc_in"), 16)
                eng.wait_ge(pj_free[3], R_IN[l] + 3)
                eng.wait_ge(sem("invc_in"), 16 * (l + 1))
                row, pad = GRID_W + 2 * POOL_PAD, POOL_PAD
                x0_, end_ = S + 2 * pad, S + 2 * pad + ROWS * (GRID_W + 2 * pad)
                first = 0 if l == 0 else x0_
                for gi in range(4):
                    w = 2 << gi
                    a_, b_ = pads
                    grid = u[:, gi, S:T].rearrange("p (r c) -> p r c", r=ROWS)
                    dst = a_[:, x0_:end_].rearrange("p (r c) -> p r c", r=ROWS)[:, :, pad:pad + GRID_W]
                    if l or gi:
                        eng.wait_ge(sem("pooled"), 4 * l + gi)
                    pool.step(eng.memset(a_[:, first:end_], 0.0))
                    if l == 0:
                        pool.mark(eng.tensor_copy(a_[:, pad:pad + S], u[:, gi, 0:S]))
                    if w <= 4:
                        pool.step(eng.tensor_copy(dst, grid))
                        pool.step(tt(dst[:, 1:4], dst[:, 1:4], grid[:, 0:3], ALU.add))
                        if w == 4:
                            pool.step(tt(dst[:, 0:3], dst[:, 0:3], grid[:, 1:4], ALU.add))
                            pool.step(tt(dst[:, 2:4], dst[:, 2:4], grid[:, 0:2], ALU.add))
                    else:
                        pool.step(tt(b_[:, 0:2 * GRID_W], u[:, gi, S:S + 2 * GRID_W], u[:, gi, S + 2 * GRID_W:T], ALU.add))
                        both = b_[:, 0:2 * GRID_W].rearrange("p (r c) -> p r c", r=2)
                        shape = [P, ROWS, GRID_W]
                        pool.step(tt(dst, both[:, 0:1, :].to_broadcast(shape), both[:, 1:2, :].to_broadcast(shape), ALU.add))
                    sh, last = 1, end_
                    while sh < w:
                        last -= sh
                        pool.step(tt(b_[:, first:last], a_[:, first:last], a_[:, first + sh:last + sh], ALU.add))
                        a_, b_ = b_, a_
                        sh *= 2
                    at_ = pad - w // 2
                    if l == 0:
                        pool.mark(tt(b_[:, 0:S], a_[:, at_:at_ + S], invc[:, gi, 0:S], ALU.mult))
                    wide = a_[:, x0_:x0_ + ROWS * row].rearrange("p (r c) -> p r c", r=ROWS)[:, :, at_:at_ + GRID_W]
                    pool.step(tt(b_[:, S:T].rearrange("p (r c) -> p r c", r=ROWS), wide,
                                 invc[:, gi, S:T].rearrange("p (r c) -> p r c", r=ROWS), ALU.mult))
                    c0 = C0[l]
                    tt(u[:, gi, c0:T], b_[:, c0:T], u[:, gi, c0:T], ALU.subtract).then_inc(sem("pooled"), 1)
                    if gi < 3:
                        pair = POOL_FROM[l] + (2 - l) * gi
                        cut_pairs(pair, min(pair + 2 - l, P_IN[l](6) + 1))

            def halves_of(x, h):
                return x.rearrange("p e (b two h) -> p (e b) two h", two=2, h=h)

            POOL_FROM = (P_IN[0](2) + 3, P_IN[1](2) + 2)
            cut_pairs(0, ADA_FIRST + 1)
            for l in range(2):
                cut_pairs(P_IN[l](0) if l == 0 else P_IN[l](0) + 1, POOL_FROM[l])
                pooling(l)
                eng.wait_ge(sem("keys_done"), 2 * l + 2)
                eng.wait_ge(sem("gate_done"), 2 * l + 2)
                for s in range(2):
                    if FULL[l, s]:
                        if (l, s) == (0, 1):
                            eng.wait_ge(mi_full, MISC[("att", 0, 0, 1, 7, 0)][1])
                        if (l, s) == (0, 0):
                            pool.mark(eng.memset(KE[0][:], 0.0))
                        tt(KE[1][:], kk[:, 0, s], kk[:, 1, s], ALU.add).then_inc(sem("diag_k"), 1)
                    for d in range(2):
                        tk = 0 if d == 0 else 1
                        for li, h in enumerate(LEVELS):
                            if not FULL[l, s]:
                                break
                            eng.wait_ge(sem("decayed"), N_EXP[l, s, d, li])
                            x = halves_of(KE[li % 2][:], h)[:, :, tk, :]
                            tt(x, x, halves_of(kk[:, d, s], h)[:, :, tk, :], ALU.mult).then_inc(sem("k_ready"), 1)
                            c = 2 * s + d
                            if li == 2 and c > (2 if l else 0):
                                cut_lo(P_IN[l](5 + c) + 1, 1)
                            if li == 6:
                                cut_lo(P_IN[l](6 + c) + 1, 0)
                        if s == 0:
                            eng.wait_ge(sem("decayed"), N_EXP[l, s, d, 8])
                            tt(KE[0][:], KE[0][:], kk[:, d, 0], ALU.mult).then_inc(sem("k_ready"), 1)
                        if not FULL[l, s]:
                            for p in range(2):
                                cut_lo(P_IN[l](6 + d) + 1, p)
                cut_lo(P_BR[l], 1)
                cut_pairs(P_BR[l] + 1, P_L1 + 1 if l == 0 else DENSE_UNITS // 2)
            eng.wait_ge(sem("jobs_ready"), 1)
            n_jobs = eng.value_load(jobs[0:1, 0:1], min_val=NE, max_val=JOBS)
            with eng.Fori(0, n_jobs) as j:
                for n in range(JU):
                    eng.wait_ge(hi_done, DENSE_UNITS + j * JU + n + 1)
                    x = (slice(None), slice(VM, 2048))
                    tt(mw_lo[n % HL_M][x], raw_m[n % RAW_M][x], mw_hi[n % HL_M][x], ALU.subtract).then_inc(lo_pool, 1)


def shape_constants():
    import numpy as np
    i = np.arange(P)
    masks = np.zeros((P, 14, P), np.float32)
    for li in range(7):
        h = 1 << li
        same = (i[:, None] // (2 * h)) == (i[None, :] // (2 * h))
        late = (i // h) % 2
        masks[:, li] = same & (late[:, None] == 0) & (late[None, :] == 1)
        masks[:, 7 + li] = same & (late[:, None] == 1) & (late[None, :] == 0)

    def counts(length, w):
        pos = np.arange(length)
        return np.clip(pos - w // 2 + w, 0, length) - np.clip(pos - w // 2, 0, length)

    inv = np.zeros((4, T), np.float32)
    for g in range(4):
        w = 2 << g
        inv[g, 0:S] = 1.0 / counts(S, w)
        inv[g, S:T] = (1.0 / np.outer(counts(ROWS, w), counts(GRID_W, w))).reshape(-1)
    sel = np.zeros((2, 2, 2, 2, 2, 2, 2), np.float32)
    for unit in range(2):
        for st in range(2):
            for h in range(2):
                sel[unit, :, st, h, unit, h, st] = 1.0
    sel = sel.reshape(8, 16)
    return {
        "k_ident": np.eye(P, dtype=np.float32),
        "k_masks": masks,
        "k_sel": sel,
        "k_ltri": (i[:, None] < i[None, :]).astype(np.float32),
        "k_iota": np.broadcast_to(i.astype(np.float32), (P, P)).copy(),
        "k_invc": np.broadcast_to(inv, (P, 4, T)).copy(),
    }


def kernel(**inputs):
    import numpy as np
    import concourse.bacc as bacc
    from concourse.bass_utils import run_bass_kernel_spmd

    arrays = {name: np.ascontiguousarray(a) for name, a in inputs.items()}
    arrays.update(shape_constants())
    nc = bacc.Bacc("TRN2", target_bir_lowering=False, num_devices=1)
    feeds, A = {}, {}
    for name, a in arrays.items():
        feeds[f"in_{name}"] = a
        A[name] = nc.dram_tensor(f"in_{name}", a.shape, mybir.dt.from_np(a.dtype), kind="ExternalInput").ap()
    A["spill"] = nc.dram_tensor("gates_spill", (16, P, T), F32, kind="Internal").ap()
    out = nc.dram_tensor("out_x", (1, S, D), F32, kind="ExternalOutput").ap()
    trunk_kernel(nc, A, out)
    r = run_bass_kernel_spmd(nc, [feeds], core_ids=[0])
    return np.asarray(r.results[0]["out_x"])
```
